# Optimizing a Trainium2 kernel written in Bass

```python
import math, functools
import jax, jax.numpy as jnp
from jax import lax
import numpy as np

D_MODEL = 2048
BATCH = 1
SEQ = 256
DEPTH = 1
DEC_BATCH = 8
DEC_SEQ = 4
PAST_LEN = 1024
PAGE_SIZE = 128

A_HEADS = 8
A_DQK = 128
A_DV = 256
A_QK_W = A_HEADS * A_DQK
A_V_W = A_HEADS * A_DV
A_CHUNK = 64
GATE_CAP = 15.0
B_HEADS = 16
B_Q_LORA = 512
B_KV_LORA = 512
B_NOPE = 128
B_ROPE = 64
B_QK = B_NOPE + B_ROPE
B_V = 128
ROPE_THETA = 10000.0
Q_BLOCK = 128
ATTN_SCALE = B_QK ** -0.5
D_FF = 5632
CONV_W = 3
EPS = 1e-6
IN_SPLITS = (A_QK_W, A_QK_W, A_V_W, A_V_W, A_HEADS, A_HEADS, B_Q_LORA, B_KV_LORA, B_ROPE, D_MODEL, D_MODEL)
D_IN = sum(IN_SPLITS)

kernel_name = 'hybrid_mlstm_mla_convffn_step'

def rmsnorm(x, g):
    x32 = x.astype(jnp.float32)
    r = lax.rsqrt(jnp.mean(x32 * x32, axis=-1, keepdims=True) + EPS)
    return (x32 * r * g.astype(jnp.float32)).astype(x.dtype)

def soft_cap(x):
    return GATE_CAP * jnp.tanh(x / GATE_CAP)

def rope(x, pos):
    half = x.shape[-1] // 2
    freqs = ROPE_THETA ** (-jnp.arange(half, dtype=jnp.float32) / half)
    ang = pos.astype(jnp.float32)[..., None] * freqs
    cos = jnp.cos(ang).astype(x.dtype)
    sin = jnp.sin(ang).astype(x.dtype)
    x1, x2 = x[..., :half], x[..., half:]
    return jnp.concatenate([x1 * cos - x2 * sin, x2 * cos + x1 * sin], axis=-1)

def qk_norm(x_nope, x_rope, g_nope, g_rope):
    x = jnp.concatenate([x_nope, x_rope], axis=-1)
    return rmsnorm(x, jnp.concatenate([g_nope, g_rope, g_rope]))

def split_cols(z):
    parts = []
    off = 0
    for w in IN_SPLITS:
        parts.append(z[..., off:off + w])
        off += w
    return parts

def project_in(x, pos, g_attn_norm, w_in, b_gates, g_q_a, w_uq, g_qk_nope_q, g_qk_rope_q, g_kv_a):
    b, s, _ = x.shape
    xn = rmsnorm(x, g_attn_norm)
    z = jnp.einsum('bsd,de->bse', xn, w_in)
    qa, ka, va, oa, ia, fa, cq, ckv, kr, gate_a, gate_b = split_cols(z)
    q_a = qa.reshape(b, s, A_HEADS, A_DQK)
    k_a = ka.reshape(b, s, A_HEADS, A_DQK) * (A_DQK ** -0.5)
    v_a = va.reshape(b, s, A_HEADS, A_DV)
    i_pre = ia + b_gates[:A_HEADS]
    f_pre = fa + b_gates[A_HEADS:]
    q_b = jnp.einsum('bsc,che->bshe', rmsnorm(cq, g_q_a), w_uq)
    q_b = qk_norm(q_b[..., :B_NOPE], rope(q_b[..., B_NOPE:], pos[:, None]), g_qk_nope_q, g_qk_rope_q)
    c_kv = rmsnorm(ckv, g_kv_a)
    k_rope = rope(kr, pos)
    return q_a, k_a, v_a, i_pre, f_pre, oa, q_b, c_kv, k_rope, gate_a, gate_b

def mlstm_chunkwise(q, k, v, log_i, log_f, C0, n0, m0, chunk):
    bsz, nh, s, _ = q.shape
    nc = s // chunk

    def chunks(t):
        return jnp.moveaxis(t.reshape(t.shape[:2] + (nc, chunk) + t.shape[3:]), 2, 0)

    causal = jnp.tril(jnp.ones((chunk, chunk), dtype=bool))

    def step(carry, xc):
        C, n, m = carry
        qc, kc, vc, li, lf = xc
        bcum = jnp.cumsum(lf, axis=-1)
        log_w = bcum[..., :, None] - bcum[..., None, :] + li[..., None, :]
        log_w = jnp.where(causal, log_w, -jnp.inf)
        log_state = bcum + m[..., None]
        m_row = jnp.maximum(log_state, jnp.max(log_w, axis=-1))
        w = jnp.exp(log_w - m_row[..., None])
        w_state = jnp.exp(log_state - m_row)
        sc = jnp.einsum('bhld,bhsd->bhls', qc, kc) * w
        num = jnp.einsum('bhls,bhsv->bhlv', sc, vc) + w_state[..., None] * jnp.einsum('bhld,bhdv->bhlv', qc, C)
        den = jnp.sum(sc, axis=-1) + w_state * jnp.einsum('bhld,bhd->bhl', qc, n)
        h = num / jnp.maximum(jnp.abs(den), jnp.exp(-m_row))[..., None]
        b_last = bcum[..., -1]
        log_k = b_last[..., None] - bcum + li
        m_new = jnp.maximum(b_last + m, jnp.max(log_k, axis=-1))
        wk = jnp.exp(log_k - m_new[..., None])
        decay = jnp.exp(b_last + m - m_new)
        kw = kc * wk[..., None]
        C_new = decay[..., None, None] * C + jnp.einsum('bhsd,bhsv->bhdv', kw, vc)
        n_new = decay[..., None] * n + jnp.sum(kw, axis=2)
        return (C_new, n_new, m_new), h

    (C, n, m), h = lax.scan(step, (C0, n0, m0), tuple(chunks(t) for t in (q, k, v, log_i, log_f)))
    h = jnp.moveaxis(h, 0, 2).reshape(bsz, nh, s, v.shape[-1])
    return h, C, n, m

def mlstm_branch(q, k, v, i_pre, f_pre, o_pre, C0, n0, m0, g_out):
    b, s, nh, _ = q.shape
    f32 = jnp.float32
    tr = lambda t: jnp.swapaxes(t, 1, 2).astype(f32)
    log_i = soft_cap(i_pre.astype(f32))
    log_f = jax.nn.log_sigmoid(soft_cap(f_pre.astype(f32)))
    hid, C, n, m = mlstm_chunkwise(tr(q), tr(k), tr(v), tr(log_i), tr(log_f),
                                   C0.astype(f32), n0.astype(f32), m0.astype(f32), math.gcd(s, A_CHUNK))
    hid = jnp.swapaxes(hid, 1, 2)
    hid = rmsnorm(hid, g_out.reshape(nh, A_DV)).reshape(b, s, nh * A_DV).astype(o_pre.dtype)
    return hid * jax.nn.sigmoid(o_pre), C, n, m

def mla_keys(c_kv, k_rope, w_uk, g_kn, g_kr):
    k_nope = jnp.einsum('...sc,chd->...shd', c_kv, w_uk)
    k_r = jnp.broadcast_to(k_rope[..., None, :], k_nope.shape[:-1] + (B_ROPE,))
    return qk_norm(k_nope, k_r, g_kn, g_kr)

def mla_attend(q, k, c_kv, mask, w_uv):
    s = jnp.einsum('bqhe,bkhe->bhqk', q, k).astype(jnp.float32) * ATTN_SCALE
    s = jnp.where(mask, s, -jnp.inf)
    p = jax.nn.softmax(s, axis=-1).astype(c_kv.dtype)
    o_lat = jnp.einsum('bhqk,bkc->bqhc', p, c_kv)
    return jnp.einsum('bqhc,chv->bqhv', o_lat, w_uv)

def mla_prompt(q, c_kv, k_rope, w_uk, w_uv, g_kn, g_kr):
    b, s = q.shape[:2]
    k = mla_keys(c_kv, k_rope, w_uk, g_kn, g_kr)
    qb = math.gcd(s, Q_BLOCK)
    k_pos = jnp.arange(s)

    def block(i):
        start = i * qb
        q_blk = lax.dynamic_slice_in_dim(q, start, qb, axis=1)
        mask = k_pos[None, :] <= (start + jnp.arange(qb))[:, None]
        return mla_attend(q_blk, k, c_kv, mask, w_uv)

    o = lax.map(block, jnp.arange(s // qb))
    return jnp.moveaxis(o, 0, 1).reshape(b, s, B_HEADS * B_V)

def mla_sample(q, c_kv_new, k_rope_new, cache_kv_latent, cache_k_rope, page_table, layer, w_uk, w_uv, g_kn, g_kr):
    bd, s = q.shape[:2]
    past = page_table.shape[1] * cache_kv_latent.shape[2]
    k_pos = jnp.arange(past + s)
    q_pos = past + jnp.arange(s)
    mask = k_pos[None, :] <= q_pos[:, None]

    def one(args):
        pt, q_seq, c_new, r_new = args
        lat = jnp.concatenate([cache_kv_latent[layer, pt].reshape(past, B_KV_LORA).astype(c_new.dtype), c_new], axis=0)
        kr = jnp.concatenate([cache_k_rope[layer, pt].reshape(past, B_ROPE).astype(r_new.dtype), r_new], axis=0)
        k = mla_keys(lat, kr, w_uk, g_kn, g_kr)
        return mla_attend(q_seq[None], k[None], lat[None], mask, w_uv)[0]

    o = lax.map(one, (page_table, q, c_kv_new, k_rope_new))
    return o.reshape(bd, s, B_HEADS * B_V)

def conv_ffn(x, prev, w_up, w_conv, b_conv, w_down):
    s = x.shape[1]
    u = jnp.einsum('bsd,df->bsf', x, w_up)
    ext = jnp.concatenate([prev.astype(u.dtype), u], axis=1)
    c = b_conv + sum(ext[:, j:j + s] * w_conv[j] for j in range(CONV_W))
    gate, val = c[..., :D_FF], c[..., D_FF:]
    out = jnp.einsum('bsf,fd->bsd', jax.nn.silu(gate) * val, w_down)
    return out, ext[:, ext.shape[1] - (CONV_W - 1):]

def layer(x, pos, C0, n0, m0, conv0, attend, g_attn_norm, w_in, b_gates, g_q_a, w_uq, g_qk_nope_q, g_qk_rope_q,
          g_kv_a, g_mlstm_out, w_branch_a, w_branch_b, w_out, g_ffn_norm, w_up, w_conv, b_conv, w_down):
    q_a, k_a, v_a, i_pre, f_pre, o_pre, q_b, c_kv, k_rope, gate_a, gate_b = project_in(
        x, pos, g_attn_norm, w_in, b_gates, g_q_a, w_uq, g_qk_nope_q, g_qk_rope_q, g_kv_a)
    h_a, C, n, m = mlstm_branch(q_a, k_a, v_a, i_pre, f_pre, o_pre, C0, n0, m0, g_mlstm_out)
    h_b = attend(q_b, c_kv, k_rope)
    merged = jax.nn.sigmoid(gate_a) * (h_a @ w_branch_a) + jax.nn.sigmoid(gate_b) * (h_b @ w_branch_b)
    x = x + merged @ w_out
    f, conv_new = conv_ffn(rmsnorm(x, g_ffn_norm), conv0, w_up, w_conv, b_conv, w_down)
    return x + f, (c_kv, k_rope, C, n, m, conv_new)

def setup_inputs(seed: int = 0) -> dict:
    key = jax.random.key(seed)
    ks = jax.random.split(key, 40)
    f32 = jnp.float32
    n_pages = PAST_LEN // PAGE_SIZE
    n_used = DEC_BATCH * n_pages
    n_pool = n_used + (n_used + 3) // 4
    nrm = lambda k, shape, s=1.0: s * jax.random.normal(k, shape, f32)
    gain = lambda k, shape: 1.0 + 0.05 * jax.random.normal(k, shape, f32)
    b_gates = jnp.concatenate([nrm(ks[10], (DEPTH, A_HEADS), 0.01), 3.0 + nrm(ks[11], (DEPTH, A_HEADS), 0.5)], axis=-1)
    page_table = jax.random.permutation(ks[9], n_pool)[:n_used].reshape(DEC_BATCH, n_pages).astype(jnp.int32)
    return {
        'x_prompt': nrm(ks[0], (BATCH, SEQ, D_MODEL)),
        'x_sample': nrm(ks[1], (DEC_BATCH, DEC_SEQ, D_MODEL)),
        'cache_kv_latent': nrm(ks[2], (DEPTH, n_pool, PAGE_SIZE, B_KV_LORA)),
        'cache_k_rope': nrm(ks[3], (DEPTH, n_pool, PAGE_SIZE, B_ROPE)),
        'state_mlstm_C': nrm(ks[4], (DEPTH, DEC_BATCH, A_HEADS, A_DQK, A_DV), 0.2),
        'state_mlstm_n': nrm(ks[5], (DEPTH, DEC_BATCH, A_HEADS, A_DQK), 0.2),
        'state_mlstm_m': jax.random.uniform(ks[6], (DEPTH, DEC_BATCH, A_HEADS), f32, 0.0, 3.0),
        'state_conv': nrm(ks[7], (DEPTH, DEC_BATCH, CONV_W - 1, 2 * D_FF)),
        'page_table': page_table,
        'g_attn_norm': gain(ks[12], (DEPTH, D_MODEL)),
        'w_in': nrm(ks[13], (DEPTH, D_MODEL, D_IN), D_MODEL ** -0.5),
        'b_gates': b_gates,
        'g_q_a': gain(ks[14], (DEPTH, B_Q_LORA)),
        'w_uq': nrm(ks[15], (DEPTH, B_Q_LORA, B_HEADS, B_QK), B_Q_LORA ** -0.5),
        'g_qk_nope_q': gain(ks[16], (DEPTH, B_NOPE)),
        'g_qk_rope_q': gain(ks[17], (DEPTH, B_ROPE // 2)),
        'g_kv_a': gain(ks[18], (DEPTH, B_KV_LORA)),
        'w_uk': nrm(ks[19], (DEPTH, B_KV_LORA, B_HEADS, B_NOPE), B_KV_LORA ** -0.5),
        'w_uv': nrm(ks[20], (DEPTH, B_KV_LORA, B_HEADS, B_V), B_KV_LORA ** -0.5),
        'g_qk_nope_k': gain(ks[21], (DEPTH, B_NOPE)),
        'g_qk_rope_k': gain(ks[22], (DEPTH, B_ROPE // 2)),
        'g_mlstm_out': gain(ks[23], (DEPTH, A_V_W)),
        'w_branch_a': nrm(ks[24], (DEPTH, A_V_W, D_MODEL), A_V_W ** -0.5),
        'w_branch_b': nrm(ks[25], (DEPTH, B_HEADS * B_V, D_MODEL), (B_HEADS * B_V) ** -0.5),
        'w_out': nrm(ks[26], (DEPTH, D_MODEL, D_MODEL), D_MODEL ** -0.5),
        'g_ffn_norm': gain(ks[27], (DEPTH, D_MODEL)),
        'w_up': nrm(ks[28], (DEPTH, D_MODEL, 2 * D_FF), D_MODEL ** -0.5),
        'w_conv': nrm(ks[29], (DEPTH, CONV_W, 2 * D_FF), CONV_W ** -0.5),
        'b_conv': nrm(ks[30], (DEPTH, 2 * D_FF), 0.01),
        'w_down': nrm(ks[31], (DEPTH, D_FF, D_MODEL), D_FF ** -0.5),
    }

def reference(x_prompt, x_sample, cache_kv_latent, cache_k_rope, state_mlstm_C, state_mlstm_n, state_mlstm_m,
              state_conv, page_table, g_attn_norm, w_in, b_gates, g_q_a, w_uq, g_qk_nope_q, g_qk_rope_q, g_kv_a,
              w_uk, w_uv, g_qk_nope_k, g_qk_rope_k, g_mlstm_out, w_branch_a, w_branch_b, w_out, g_ffn_norm,
              w_up, w_conv, b_conv, w_down):
    f32 = jnp.float32
    bp, s_p, _ = x_prompt.shape
    s_s = x_sample.shape[1]
    past = page_table.shape[1] * cache_kv_latent.shape[2]
    pos_p = jnp.arange(s_p, dtype=jnp.int32)
    pos_s = past + jnp.arange(s_s, dtype=jnp.int32)
    hp, hs = x_prompt, x_sample
    new_p, new_s = [], []
    for l in range(DEPTH):
        wl = (g_attn_norm[l], w_in[l], b_gates[l], g_q_a[l], w_uq[l], g_qk_nope_q[l], g_qk_rope_q[l], g_kv_a[l],
              g_mlstm_out[l], w_branch_a[l], w_branch_b[l], w_out[l], g_ffn_norm[l], w_up[l], w_conv[l], b_conv[l],
              w_down[l])
        attend_p = functools.partial(mla_prompt, w_uk=w_uk[l], w_uv=w_uv[l], g_kn=g_qk_nope_k[l], g_kr=g_qk_rope_k[l])
        attend_s = functools.partial(mla_sample, cache_kv_latent=cache_kv_latent, cache_k_rope=cache_k_rope,
                                     page_table=page_table, layer=l, w_uk=w_uk[l], w_uv=w_uv[l],
                                     g_kn=g_qk_nope_k[l], g_kr=g_qk_rope_k[l])
        C0 = jnp.zeros((bp, A_HEADS, A_DQK, A_DV), f32)
        n0 = jnp.zeros((bp, A_HEADS, A_DQK), f32)
        m0 = jnp.zeros((bp, A_HEADS), f32)
        conv0 = jnp.zeros((bp, CONV_W - 1, 2 * D_FF), x_prompt.dtype)
        hp, st_p = layer(hp, pos_p, C0, n0, m0, conv0, attend_p, *wl)
        hs, st_s = layer(hs, pos_s, state_mlstm_C[l], state_mlstm_n[l], state_mlstm_m[l], state_conv[l], attend_s, *wl)
        new_p.append(st_p)
        new_s.append(st_s)
    dts = (cache_kv_latent.dtype, cache_k_rope.dtype, state_mlstm_C.dtype, state_mlstm_n.dtype,
           state_mlstm_m.dtype, state_conv.dtype)
    stk = lambda lst, i: jnp.stack([st[i] for st in lst], axis=0).astype(dts[i])
    kv_latent_p, k_rope_p, mlstm_C_p, mlstm_n_p, mlstm_m_p, conv_p = [stk(new_p, i) for i in range(6)]
    kv_latent_s, k_rope_s, mlstm_C_s, mlstm_n_s, mlstm_m_s, conv_s = [stk(new_s, i) for i in range(6)]
    return (hp, hs, kv_latent_p, k_rope_p, mlstm_C_p, mlstm_n_p, mlstm_m_p, conv_p,
            kv_latent_s, k_rope_s, mlstm_C_s, mlstm_n_s, mlstm_m_s, conv_s)


_drawn_inputs = setup_inputs


def setup_inputs(seed=0):
    import zlib

    import numpy as np

    out = dict(_drawn_inputs(seed))
    spreads = {}
    factors = {'cache_k_rope': 3.895,
     'g_q_a': 8.0,
     'g_qk_nope_q': 8.0,
     'g_qk_rope_q': 8.0,
     'g_qk_nope_k': 8.0,
     'g_qk_rope_k': 8.0,
     'g_mlstm_out': 3.666,
     'b_conv': 7.969}
    for name, (base, spread) in spreads.items():
        noise = np.random.default_rng([zlib.crc32(name.encode()), seed]).standard_normal(out[name].shape)
        drawn = base * np.exp(spread * noise) if base else spread * noise
        out[name] = __import__('jax').numpy.asarray(drawn.astype(out[name].dtype))
    for name, factor in factors.items():
        out[name] = (out[name] * factor).astype(out[name].dtype)
    return out
```

```python
from contextlib import ExitStack

import numpy as np
import concourse.bass as bass
from concourse import mybir

F32 = mybir.dt.float32
F32R = mybir.dt.float32r
I32 = mybir.dt.int32
ALU = mybir.AluOpType
ACT = mybir.ActivationFunctionType
AX = mybir.AxisListType

P = 128
D = 2048
KC = D // P
S_P, NB, S_S = 256, 8, 4
N_S = NB * S_S
T = S_P + N_S
TILES = [(0, 128), (128, 128), (256, 32)]
PAST, PAGE = 1024, 128
NPG = PAST // PAGE
NPOOL = 80
AH, DQK, DV = 8, 128, 256
BH, QL, KVL, NOPE, ROPE, BV = 16, 512, 512, 128, 64, 128
LC = KVL // P
BQK = NOPE + ROPE
SCALE = BQK ** -0.5
CAP = 15.0
FF = 5632
FC = FF // P
CW = 3
EPS = 1e-6
NEG = -1e30
O_Q, O_K, O_V, O_O = 0, 1024, 2048, 4096
O_I, O_CQ, O_CKV, O_KR, O_GA, O_GB = 6144, 6160, 6672, 7184, 7248, 9296
GRP = FC // 2
KD = GRP // 2


class At:

    def __init__(self, c, step=0, i=None):
        self.c, self.step, self.i = c, step, i

    def __add__(self, k):
        return At(self.c + k, self.step, self.i)

    def __sub__(self, k):
        return self + (-k)

    def of(self, mul=1, add=0):
        if self.i is None:
            return self.c * mul + add
        return self.i * (self.step * mul) + (self.c * mul + add)

    def div(self, n, add=0, mul=1):
        if self.i is None:
            return (self.c // n + add) * mul
        return self.i * (self.step // n * mul) + (self.c // n + add) * mul

    def mod(self, n):
        return self.c % n


def need(eng, sem, value):
    if isinstance(value, int) and value < 1:
        return
    eng.wait_ge(sem, value)


class Own:

    def __init__(self, sem):
        self.sem, self.count = sem, At(0)

    def step(self, eng, ins):
        ins.then_inc(self.sem, 1)
        self.count = self.count + 1
        eng.wait_ge(self.sem, self.count.of())

    def enter(self, i, per):
        self.base, self.per = self.count.c, per
        self.count = At(self.base, per, i)

    def leave(self, times):
        assert self.count.c == self.base + self.per, (self.count.c - self.base, self.per)
        self.count = At(self.base + self.per * times)


def constants():
    parts, at, n = [], {}, 0

    def put(name, a):
        nonlocal n
        a = np.asarray(a, np.float32)
        a = a.reshape(a.shape[0], -1)
        full = np.zeros((P, a.shape[1]), np.float32)
        full[: a.shape[0]] = a
        at[name] = (n, a.shape[0], a.shape[1])
        parts.append(full)
        n += a.shape[1]

    r = np.arange(P)
    q, s = r[None, :], r[:, None]
    put("ident", np.eye(P))
    put("ones", np.ones((P, P)))
    put("seen_t", np.concatenate([np.where(q >= s, 0, NEG), np.zeros((P, P))], 1))
    tri = np.where(r[None, :] <= r[:, None], 0, NEG)
    put("seen", np.concatenate([tri, np.zeros((P, P)), tri], 1))
    put("upto", (s <= q) * 1.0)
    r = np.arange(N_S)
    q, s = r[None, :], r[:, None]
    same = q // S_S == s // S_S
    put("upto_s", (same & (s <= q)) * 1.0)
    put("same_s", same * 1.0)
    put("seen_t_s", np.where(same & (s <= q), 0, NEG))
    put("seen_s", np.where(same & (q <= s), 0, NEG))
    put("same_neg", np.where(same, 0, NEG))
    b = np.arange(NB)
    put("of_b", (r[:, None] // S_S == b[None, :]) * 1.0)
    put("first_of_b", (r[:, None] == S_S * b[None, :]) * 1.0)
    put("cols_of_b", np.broadcast_to((r[None, None, :] // S_S == b[None, :, None]) * 1.0, (P, NB, N_S)))
    put("pick", np.broadcast_to(np.eye(AH)[:, :, None], (AH, AH, P)))
    st = np.arange(S_S)
    put("new_seen", np.where((r[:, None, None] // S_S == b[None, :, None])
                             & (r[:, None, None] % S_S <= st[None, None, :]), 0, NEG))
    half = ROPE // 2
    freq = (np.float32(10000.0) ** (-np.arange(half, dtype=np.float32) / np.float32(half))).astype(np.float32)
    pos = np.zeros((P, 3))
    pos[:, 0], pos[:, 1] = np.arange(P), P + np.arange(P)
    pos[:N_S, 2] = PAST + np.arange(N_S) % S_S
    ang = (pos.astype(np.float32)[:, :, None] * freq).astype(np.float32)
    put("cos", np.cos(ang.astype(np.float64)))
    put("sin", np.sin(ang.astype(np.float64)))
    put("eps", np.full((P, 1), EPS))
    return np.concatenate(parts, 1), at


def build(nc, A, O):
    ctx = ExitStack()

    def sb(stack, name, shape, dt=F32):
        return stack.enter_context(nc.sbuf_tensor(name, shape, dt))

    def lasting(name):
        return ctx.enter_context(nc.semaphore(name))

    phase_sems = []

    def sem(name):
        phase_sems.append(nc.alloc_semaphore(name=name))
        return phase_sems[-1]

    def recycle():
        nc.clear_and_free_semaphores(phase_sems)
        nc.all_engine_barrier()
        phase_sems.clear()

    table, where = constants()
    table_dram = nc.inline_tensor(table, "shape_tables").ap()
    xT_dram = nc.dram_tensor("xT_scratch", (P, KC, T), F32, kind="Internal").ap()
    hb_dram = nc.dram_tensor("hb_scratch", (P, BH, T), F32, kind="Internal").ap()

    with ctx:
        bank = [ctx.enter_context(nc.psum_tensor(f"bank{i}", [P, 512], F32)) for i in range(8)]
        cst = sb(ctx, "cst", [P, table.shape[1]])
        vec = sb(ctx, "vec", [P, 60])
        gate_tok = sb(ctx, "gate_tok", [P, 3, 2 * AH])
        xnH = sb(ctx, "xnH", [P, KC, T], F32R)
        xnL = sb(ctx, "xnL", [P, KC, T], F32R)
        stage = sb(ctx, "stage", [P, 4, KC * P])

        def C(name, rows=None):
            o, r, n = where[name]
            return cst[0:(rows or r), o:o + n]

        ident = C("ident")
        ones = C("ones")
        eps = C("eps")
        G_ATTN, G_FFN, G_ML, G_QA, G_KVA, G_NQ, G_NK, G_RQ, G_RK = 0, 16, 32, 48, 52, 56, 57, 58, 59

        cst_in = lasting("cst_in")
        stored = lasting("stored")
        n_stored = [0]

        def store(eng, dst, src, add=1):
            n_stored[0] += add
            return eng.dma_start(dst, src).then_inc(stored, 16)

        def all_stored(eng):
            eng.wait_ge(stored, 16 * n_stored[0])

        pe_own, act_own, dve_own, pool_own = (Own(lasting(f"{x}_own")) for x in ("pe", "act", "dve", "pool"))

        w_in_v = A["w_in"][0].rearrange("(k p) n -> p k n", p=P)
        wa_v = A["w_branch_a"][0].rearrange("(k p) n -> p k n", p=P)
        wb_v = A["w_branch_b"][0].rearrange("(k p) n -> p k n", p=P)
        wo_v = A["w_out"][0].rearrange("(k p) n -> p k n", p=P)
        up_v = A["w_up"][0].rearrange("(k p) n -> p k n", p=P)
        down_v = A["w_down"][0].rearrange("(k p) n -> p k n", p=P)
        w_landed = [lasting(f"w_landed{s}") for s in range(4)]
        w_hi = lasting("w_hi")
        w_lo = lasting("w_lo")
        w_done = lasting("w_done")
        z_free = [lasting(f"z_free{s}") for s in range(4)]

        def w_load(sp, n, view, col, width=P, k0=0, kc=KC):
            need(sp, w_lo, n.of(1, -3))
            slot = stage[:, n.mod(4), :].rearrange("p (k m) -> p k m", m=P)
            src = view[:, k0:k0 + kc, bass.ds(col, width)] if not isinstance(k0, tuple) else None
            sp.dma_start(slot[:, 0:kc, 0:width], src).then_inc(w_landed[n.mod(4)], 16)

        def split_hi(act, n, width=P, kc=KC):
            need(act, w_landed[n.mod(4)], n.div(4, 1, 16))
            need(act, w_done, n.of(1, -1))
            a = stage[:, n.mod(4), :].rearrange("p (k m) -> p k m", m=P)[:, 0:kc, 0:width]
            h = ws["hi"][:, n.mod(2), :].rearrange("p (k m) -> p k m", m=P)[:, 0:kc, 0:width]
            act.activation(h, a, ACT.Copy).then_inc(w_hi, 1)

        def split_lo(dve, n, width=P, kc=KC):
            need(dve, w_hi, n.of(1, 1))
            a = stage[:, n.mod(4), :].rearrange("p (k m) -> p k m", m=P)[:, 0:kc, 0:width]
            h = ws["hi"][:, n.mod(2), :].rearrange("p (k m) -> p k m", m=P)[:, 0:kc, 0:width]
            lo = ws["lo"][:, n.mod(2), :].rearrange("p (k m) -> p k m", m=P)[:, 0:kc, 0:width]
            dve.tensor_tensor(lo, a, h.bitcast(F32), ALU.subtract).then_inc(w_lo, 1)

        def block(pe, n, z, xH, xL, width=P, kc=KC, first=True, last=True):
            need(pe, w_lo, n.of(1, 1))
            if first:
                need(pe, z_free[z.mod(4)], z.div(4))
            out = bank[z.mod(4)][0:width, 0:T]
            for k in range(kc):
                hi = ws["hi"][:, n.mod(2), k * P:k * P + width]
                lo = ws["lo"][:, n.mod(2), k * P:k * P + width]
                pe.matmul(out, hi, xH(k), start=first and k == 0, stop=False)
                pe.matmul(out, hi, xL(k), start=False, stop=False)
                mm = pe.matmul(out, lo, xH(k), start=False, stop=last and k == kc - 1)
            mm.then_inc(w_done, 1)

        ws = {}
        N0 = 9

        with ExitStack() as ph:
            rows = sb(ph, "gain_rows", [60, P])
            rows_zero, rows_in, rows_t = sem("rows_zero"), sem("rows_in"), sem("rows_t")
            with nc.Block() as blk:
                @blk.sync
                def _(sp):
                    sp.dma_start(cst[:], table_dram).then_inc(cst_in, 16)
                    sp.wait_ge(rows_zero, 1)
                    for name, r0, nr in (("g_attn_norm", G_ATTN, 16), ("g_ffn_norm", G_FFN, 16), ("g_mlstm_out", G_ML, 16),
                                         ("g_q_a", G_QA, 4), ("g_kv_a", G_KVA, 4), ("g_qk_nope_q", G_NQ, 1), ("g_qk_nope_k", G_NK, 1)):
                        sp.dma_start(rows[r0:r0 + nr, :], A[name][0].rearrange("(c p) -> c p", p=P)).then_inc(rows_in, 16)
                    for name, r in (("g_qk_rope_q", G_RQ), ("g_qk_rope_k", G_RK)):
                        for h in range(2):
                            sp.dma_start(rows[r:r + 1, 32 * h:32 * h + 32], A[name]).then_inc(rows_in, 16)

                @blk.vector
                def _(dve):
                    dve.memset(rows[:], 0.0).then_inc(rows_zero, 1)
                    dve.wait_ge(rows_t, 1)
                    dve.tensor_copy(vec[:], bank[0][:, 0:60])

                @blk.tensor
                def _(pe):
                    pe.wait_ge(cst_in, 16)
                    pe.wait_ge(rows_in, 16 * 11)
                    pe.transpose(bank[0][:, 0:60], rows[:], ident[0:60, 0:60]).then_inc(rows_t, 1)

        kept = ctx.enter_context(ExitStack())
        rk = sb(kept, "rk", [P, NB * NPG, BH])
        page = sb(kept, "page", [1, NB * NPG], I32)
        page_in = sem("page_in")
        lat_v = A["cache_kv_latent"][0]
        kr_v = A["cache_k_rope"][0]
        with ExitStack() as ph:
            ukH = sb(ph, "ukH", [P, LC, BH * NOPE], F32R)
            ukL = sb(ph, "ukL", [P, LC, BH * NOPE], F32R)
            lat = sb(ph, "lat_n", [P, 4, KVL + ROPE])
            latH = sb(ph, "latH", [P, 2, KVL], F32R)
            latL = sb(ph, "latL", [P, 2, KVL], F32R)
            sq = sb(ph, "sq_n", [P, 4, 512])
            sqr = sb(ph, "sqr_n", [P, 4, ROPE])
            ss = sb(ph, "ss_n", [P, NB * NPG, BH])
            ssr = sb(ph, "ssr_n", [P, NB * NPG])
            uk_in, uk_hi, uk_lo = sem("uk_in"), sem("uk_hi"), sem("uk_lo")
            lat_in = [sem(f"lat_in{s}") for s in range(4)]
            n_t, n_hi, n_lo, n_k, n_sq, n_red = (sem("n_" + x) for x in ("t", "hi", "lo", "k", "sq", "red"))
            n_sum, n_rt = sem("n_sum"), sem("n_rt")
            NT = NB * NPG
            with nc.Block() as blk:
                @blk.sync
                def _(sp):
                    sp.dma_start(page[:], A["page_table"].rearrange("b j -> (b j)").rearrange("(o n) -> o n", o=1)).then_inc(page_in, 16)
                    for k in range(LC):
                        sp.dma_start(stage[:, k, :], A["w_uk"][0, k * P:(k + 1) * P].rearrange("c h d -> c (h d)")).then_inc(uk_in, 16)
                    sp.wait_ge(page_in, 16)

                    def tiles(t0):
                        for s in range(4):
                            t = t0 + s
                            v = sp.value_load(page[0:1, bass.ds(t.of(), 1)], min_val=0, max_val=NPOOL - 1)
                            need(sp, n_hi, t.of(1, -3))
                            sp.dma_start(lat[:, s, 0:KVL], lat_v[bass.ds(v, 1)].rearrange("o p c -> (o p) c")).then_inc(lat_in[s], 16)
                            sp.dma_start(lat[:, s, KVL:], kr_v[bass.ds(v, 1)].rearrange("o p c -> (o p) c")).then_inc(lat_in[s], 16)
                    tiles(At(0))
                    with sp.Fori(1, NT // 4) as i:
                        tiles(At(0, 4, i))

                @blk.tensor
                def _(pe):
                    def turn(t):
                        need(pe, lat_in[t.mod(4)], t.div(4, 1, 32))
                        need(pe, n_lo, t.of(1, -1))
                        for k in range(LC):
                            tr = pe.transpose(bank[4 + t.mod(2)][:, k * P:(k + 1) * P], lat[:, t.mod(4), k * P:(k + 1) * P], ident)
                        tr.then_inc(n_t, 1)

                    def keys(t):
                        need(pe, n_lo, t.of(1, 1))
                        for g in range(4):
                            need(pe, n_sq, t.of(4, g - 3))
                            cols = slice(g * 512, (g + 1) * 512)
                            for k in range(LC):
                                h, lo = latH[:, t.mod(2), k * P:(k + 1) * P], latL[:, t.mod(2), k * P:(k + 1) * P]
                                pe.matmul(bank[g][:], h, ukH[:, k, cols], start=k == 0, stop=False)
                                pe.matmul(bank[g][:], h, ukL[:, k, cols], start=False, stop=False)
                                mm = pe.matmul(bank[g][:], lo, ukH[:, k, cols], start=False, stop=k == LC - 1)
                            mm.then_inc(n_k, 1)
                    turn(At(0))
                    pe.wait_ge(uk_lo, LC)

                    def tiles(t0, last=False):
                        for s in range(4):
                            if not (last and s == 3):
                                turn(t0 + (s + 1))
                            keys(t0 + s)
                    tiles(At(0))
                    with pe.Fori(1, NT // 4 - 1) as i:
                        tiles(At(0, 4, i))
                    tiles(At(NT - 4), True)

                @blk.scalar
                def _(act):
                    act.wait_ge(uk_in, 16 * LC)
                    for k in range(LC):
                        act.activation(ukH[:, k, :], stage[:, k, :], ACT.Copy).then_inc(uk_hi, 1)

                    def hi(t):
                        need(act, n_t, t.of(1, 1))
                        need(act, n_hi, t.of(1, -3))
                        act.activation(sqr[:, t.mod(4), :], lat[:, t.mod(4), KVL:], ACT.Square, accum_out=ssr[:, bass.ds(t.of(), 1)])
                        need(act, n_k, t.of(4, -4))
                        act.activation(latH[:, t.mod(2), :], bank[4 + t.mod(2)][:], ACT.Copy).then_inc(n_hi, 1)

                    def squares(t):
                        for g in range(4):
                            need(act, n_k, t.of(4, g + 1))
                            need(act, n_red, t.of(4, g - 3))
                            act.activation(sq[:, g, :], bank[g][:], ACT.Square).then_inc(n_sq, 1)
                    hi(At(0))

                    def tiles(t0, last=False):
                        for s in range(4):
                            if not (last and s == 3):
                                hi(t0 + (s + 1))
                            squares(t0 + s)
                    tiles(At(0))
                    with act.Fori(1, NT // 4 - 1) as i:
                        tiles(At(0, 4, i))
                    tiles(At(NT - 4), True)
                    act.wait_ge(n_sum, 1)
                    act.activation(ss[:], ss[:], ACT.Sqrt, scale=1.0 / BQK, bias=eps).then_inc(n_rt, 1)

                @blk.vector
                def _(dve):
                    for k in range(LC):
                        dve.wait_ge(uk_hi, k + 1)
                        dve.tensor_tensor(ukL[:, k, :], stage[:, k, :], ukH[:, k, :].bitcast(F32), ALU.subtract).then_inc(uk_lo, 1)

                    def lo(t):
                        need(dve, n_hi, t.of(1, 1))
                        dve.tensor_tensor(latL[:, t.mod(2), :], bank[4 + t.mod(2)][:], latH[:, t.mod(2), :].bitcast(F32),
                                          ALU.subtract).then_inc(n_lo, 1)

                    def sums(t):
                        for g in range(4):
                            need(dve, n_sq, t.of(4, g + 1))
                            dve.tensor_reduce(ss[:, bass.ds(t.of(), 1), g * 4:g * 4 + 4].rearrange("p o h -> p (o h)"),
                                              sq[:, g, :].rearrange("p (h d) -> p h d", d=NOPE), AX.X, ALU.add).then_inc(n_red, 1)
                    lo(At(0))

                    def tiles(t0, last=False):
                        for s in range(4):
                            if not (last and s == 3):
                                lo(t0 + (s + 1))
                            sums(t0 + s)
                    tiles(At(0))
                    with dve.Fori(1, NT // 4 - 1) as i:
                        tiles(At(0, 4, i))
                    tiles(At(NT - 4), True)
                    dve.wait_ge(n_red, 4 * NT)
                    dve.tensor_tensor(ss[:], ss[:], ssr[:].unsqueeze(2).broadcast_to([P, NT, BH]), ALU.add).then_inc(n_sum, 1)
                    dve.wait_ge(n_rt, 1)
                    dve.reciprocal(rk[:], ss[:])
        ckvT = sb(kept, "ckvT", [P, LC, T])
        cqT = sb(kept, "cqT", [P, LC, T])
        zkr = sb(kept, "zkr", [ROPE + 2 * AH, T])

        nm = {x: lasting("nm_" + x) for x in ("sq", "sum", "rt", "r", "y", "hi", "lo")}
        nm_calls = [0]

        def norm_parts(ph, tag):
            return dict(sq=sb(ph, "sq" + tag, [P, 2, T]), r=sb(ph, "r" + tag, [P, T]), y=sb(ph, "y" + tag, [P, 2, T]))

        class Norm:

            def __init__(self, buf, src, nch, gain, psum, H, L):
                self.c0 = nm_calls[0]
                nm_calls[0] += nch
                self.k0 = Norm.calls
                Norm.calls += 1
                self.buf, self.src, self.n, self.gain, self.ps, self.H, self.L = buf, src, nch, gain, psum, H, L

            def add(self, pe, c):
                pe.wait_ge(nm["sq"], self.c0 + c + 1)
                pe.matmul(self.ps[:, 0:T], ones, self.buf["sq"][:, c % 2, :], start=c == 0,
                          stop=c == self.n - 1).then_inc(nm["sum"], 1)

            def tensor(self, pe):
                for c in range(self.n):
                    self.add(pe, c)

            def scalar(self, act, ready=lambda c: None):
                for c in range(self.n):
                    ready(c)
                    if c >= 2:
                        act.wait_ge(nm["sum"], self.c0 + c - 1)
                    act.activation(self.buf["sq"][:, c % 2, :], self.src[:, c, :], ACT.Square).then_inc(nm["sq"], 1)
                act.wait_ge(nm["sum"], self.c0 + self.n)
                need(act, nm["y"], self.c0)
                act.activation(self.buf["r"][:], self.ps[:, 0:T], ACT.Sqrt, scale=1.0 / (self.n * P), bias=eps).then_inc(nm["rt"], 1)
                if self.H is not None:
                    for c in range(self.n):
                        act.wait_ge(nm["y"], self.c0 + c + 1)
                        act.activation(self.H[:, c, :], self.buf["y"][:, c % 2, :], ACT.Copy).then_inc(nm["hi"], 1)

            def vector(self, dve):
                dve.wait_ge(nm["rt"], self.k0 + 1)
                dve.reciprocal(self.buf["r"][:], self.buf["r"][:]).then_inc(nm["r"], 1)
                dve.wait_ge(nm["r"], self.k0 + 1)
                for c in range(self.n):
                    if self.H is not None:
                        if c >= 2:
                            dve.wait_ge(nm["lo"], self.lo0() + c - 1)
                        dst = self.buf["y"][:, c % 2, :]
                    else:
                        dst = self.src[:, c, :]
                    dve.scalar_tensor_tensor(dst, self.src[:, c, :], vec[:, self.gain + c:self.gain + c + 1], self.buf["r"][:],
                                             ALU.mult, ALU.mult).then_inc(nm["y"], 1)
                    if self.H is not None and c >= 1:
                        self.low(dve, c - 1)
                if self.H is not None:
                    self.low(dve, self.n - 1)

            def lo0(self):
                return self.h0

            def low(self, dve, c):
                dve.wait_ge(nm["hi"], self.h0 + c + 1)
                dve.tensor_tensor(self.L[:, c, :], self.buf["y"][:, c % 2, :], self.H[:, c, :].bitcast(F32), ALU.subtract).then_inc(nm["lo"], 1)

        Norm.calls = 0
        splits = [0]

        def norm(buf, src, nch, gain, psum, H=None, L=None):
            x = Norm(buf, src, nch, gain, psum, H, L)
            x.h0 = splits[0]
            if H is not None:
                splits[0] += nch
            return x

        sm_v = A["w_in"][0].rearrange("(k p) n -> p k n", p=P)

        def small_load(sp, n):
            if n == 0:
                slot = stage[:, 0, :].rearrange("p (k m) -> p k m", m=P)
                sp.dma_start(slot[:, :, 0:ROPE], sm_v[:, :, O_KR:O_KR + ROPE]).then_inc(w_landed[0], 16)
                sp.dma_start(slot[:, :, ROPE:ROPE + 2 * AH], sm_v[:, :, O_I:O_I + 2 * AH]).then_inc(gates_in, 16)
            else:
                w_load(sp, At(n), w_in_v, (O_CQ if n <= 4 else O_CKV) + (n - 1) % 4 * P)

        gates_in = sem("gates_in")
        x_in, x_t, x_copied, x_ready = sem("x_in"), sem("x_t"), sem("x_copied"), sem("x_ready")
        W0 = ROPE + 2 * AH
        with ExitStack() as ph:
            ws["hi"] = sb(ph, "w_hi_a", [P, 2, KC * P], F32R)
            ws["lo"] = sb(ph, "w_lo_a", [P, 2, KC * P], F32R)
            xT = sb(ph, "xT", [P, KC, T])
            x_tok = sb(ph, "x_tok", [P, 3, D])
            buf = norm_parts(ph, "_x")
            nx = norm(buf, xT, KC, G_ATTN, bank[7], xnH, xnL)
            nq = norm(buf, cqT, LC, G_QA, bank[6])
            nkv = norm(buf, ckvT, LC, G_KVA, bank[5])
            with nc.Block() as blk:
                @blk.sync
                def _(sp):
                    sp.dma_start(x_tok[:, 0:2, :], A["x_prompt"][0].rearrange("(t p) d -> p t d", p=P)).then_inc(x_in, 16)
                    sp.dma_start(x_tok[0:N_S, 2, :], A["x_sample"].rearrange("b s d -> (b s) d")).then_inc(x_in, 16)
                    for n in range(9):
                        small_load(sp, n)
                    sp.wait_ge(x_copied, KC)
                    store(sp, xT_dram, xT[:])
                    all_stored(sp)

                @blk.tensor
                def _(pe):
                    pe.wait_ge(x_in, 32)
                    for c in range(KC):
                        if c >= 3:
                            pe.wait_ge(x_copied, c - 2)
                        for t, (t0, n) in enumerate(TILES):
                            tr = pe.transpose(bank[4 + c % 3][:, t0:t0 + n], x_tok[0:n, t, c * P:(c + 1) * P], ident[0:n, 0:n])
                        tr.then_inc(x_t, 1)
                        if c >= 1:
                            nx.add(pe, c - 1)
                    nx.add(pe, KC - 1)
                    pe.wait_ge(nm["lo"], KC)
                    for n in range(9):
                        block(pe, At(n), At(n), lambda k: xnH[:, k, :], lambda k: xnL[:, k, :], width=W0 if n == 0 else P)
                    nq.tensor(pe)
                    nkv.tensor(pe)

                @blk.scalar
                def _(act):
                    def copied(c):
                        act.wait_ge(x_t, c + 1)
                        act.activation(xT[:, c, :], bank[4 + c % 3][:, 0:T], ACT.Copy).then_inc(x_copied, 1)
                        act.wait_ge(x_copied, c + 1)
                    nx.scalar(act, copied)
                    act.wait_ge(gates_in, 16)
                    for n in range(10):
                        if n < 9:
                            split_hi(act, At(n), width=W0 if n == 0 else P)
                        m = n - 1
                        if m >= 0:
                            act.wait_ge(w_done, m + 1)
                            if m == 0:
                                act.activation(zkr[:], bank[0][0:W0, 0:T], ACT.Copy).then_inc(z_free[0], 1)
                            else:
                                dst = cqT[:, m - 1, :] if m <= 4 else ckvT[:, m - 5, :]
                                act.activation(dst, bank[m % 4][:, 0:T], ACT.Copy).then_inc(z_free[m % 4], 1)

                    def evacuated(base):
                        def ready(c):
                            m = base + c
                            act.wait_ge(z_free[m % 4], m // 4 + 1)
                        return ready
                    nq.scalar(act, evacuated(1))
                    nkv.scalar(act, evacuated(5))

                @blk.vector
                def _(dve):
                    nx.vector(dve)
                    for n in range(9):
                        split_lo(dve, At(n), width=W0 if n == 0 else P)
                    nq.vector(dve)
                    nkv.vector(dve)
        qrT = sb(kept, "qrT", [ROPE, BH, T])
        qlat = sb(kept, "qlat", [P, LC, NB, BH, S_S])
        c_tok = sb(kept, "c_tok", [P, 3, KVL])
        krr = sb(kept, "krr", [P, 3, ROPE])
        rk_new = sb(kept, "rk_new", [P, BH])
        heads = kept.enter_context(ExitStack())
        qT = sb(heads, "qT", [P, BH, T])
        KT = sb(heads, "KT", [P, BH, S_P])
        krT = sb(heads, "krT", [ROPE, BH, S_P])
        GW = 2 * BQK
        with ExitStack() as ph:
            uq = sb(ph, "uq", [P, 2, LC, GW])
            q_tok = sb(ph, "q_tok", [P, 2, 3, 2, BQK])
            sqq = sb(ph, "sqq", [P, 3, 2, BQK])
            rot = sb(ph, "rot", [P, 4, 3, 2, ROPE // 2])
            rq = sb(ph, "rq", [P, 2, 6])
            gq = sb(ph, "gq", [P, 2])
            krg = sb(ph, "krg", [P, 3, W0])
            uq_in = [sem("uq_in0"), sem("uq_in1")]
            (q_mm, q_ev, q_m4, q_dif, q_rot, q_sq, q_ss, q_rt, q_rc, q_nrm, q_t, q_tev, q_zero) = (
                sem("q_" + x) for x in ("mm", "ev", "m4", "dif", "rot", "sq", "ss", "rt", "rc", "nrm", "t", "tev", "zero"))
            c_t, c_ev, c_rot = sem("c_t"), sem("c_ev"), sem("c_rot")
            uq_v = A["w_uq"][0].rearrange("(k p) h e -> p k (h e)", p=P)
            cos, sin = (C(x).rearrange("p (t d) -> p t d", t=3) for x in ("cos", "sin"))
            h2 = ROPE // 2
            NG = BH // 2
            kv_p = O["kv_latent_p"][0, 0].rearrange("(t p) c -> p t c", p=P)
            kr_p = O["k_rope_p"][0, 0].rearrange("(t p) c -> p t c", p=P)
            kv_s = O["kv_latent_s"][0].rearrange("b s c -> (b s) c")
            kr_s = O["k_rope_s"][0].rearrange("b s c -> (b s) c")
            with nc.Block() as blk:
                @blk.sync
                def _(sp):
                    def load(g):
                        need(sp, q_mm, g.of(1, -1))
                        sp.dma_start(uq[:, g.mod(2)], uq_v[:, :, bass.ds(g.of() * GW, GW)]).then_inc(uq_in[g.mod(2)], 16)
                    load(At(0))
                    load(At(1))
                    for k in range(LC):
                        sp.dma_start(stage[:, k, :], A["w_uk"][0, k * P:(k + 1) * P].rearrange("c h d -> c (h d)")).then_inc(uk_in, 16)
                    with sp.Fori(1, NG // 2) as i:
                        for s in range(2):
                            load(At(s, 2, i))
                    sp.wait_ge(c_ev, 6)
                    store(sp, kv_p, c_tok[:, 0:2, :])
                    store(sp, kv_s, c_tok[0:N_S, 2, :])
                    sp.wait_ge(q_dif, 2)
                    store(sp, kr_p, krr[:, 0:2, :])
                    store(sp, kr_s, krr[0:N_S, 2, :])
                    all_stored(sp)

                @blk.tensor
                def _(pe):
                    for t, (t0, n) in enumerate(TILES):
                        tr = pe.transpose(bank[6][0:n, t * W0:(t + 1) * W0], zkr[:, t0:t0 + n], ident[0:W0, 0:W0])
                    tr.then_inc(c_t, 1)
                    for t, (t0, n) in enumerate(TILES):
                        for k in range(LC):
                            tr = pe.transpose(bank[3 + t][0:n, k * P:(k + 1) * P], ckvT[:, k, t0:t0 + n], ident)
                        tr.then_inc(c_t, 1)

                    def queries(g):
                        pe.wait_ge(uq_in[g.mod(2)], g.div(2, 1, 16))
                        if g.i is None and g.c == 1:
                            pe.wait_ge(c_ev, 6)
                        for t, (t0, n) in enumerate(TILES):
                            need(pe, q_ev, g.of(3, t - 5))
                            for k in range(LC):
                                mm = pe.matmul(bank[3 * g.mod(2) + t][0:n, 0:GW], cqT[:, k, t0:t0 + n], uq[:, g.mod(2), k, :],
                                               start=k == 0, stop=k == LC - 1)
                        mm.then_inc(q_mm, 1)

                    def turn(g):
                        pe.wait_ge(q_nrm, g.of(1, 1))
                        for a in range(2):
                            need(pe, q_tev, g.of(4, 2 * a))
                            for t, (t0, n) in enumerate(TILES):
                                tr = pe.transpose(bank[6][:, t0:t0 + n], q_tok[0:n, g.mod(2), t, a, 0:NOPE], ident[0:n, 0:n])
                            tr.then_inc(q_t, 1)
                            for t, (t0, n) in enumerate(TILES):
                                tr = pe.transpose(bank[7][0:ROPE, t0:t0 + n], q_tok[0:n, g.mod(2), t, a, NOPE:], ident[0:n, 0:n])
                            tr.then_inc(q_t, 1)
                    queries(At(0))
                    pe.wait_ge(c_ev, 6)

                    def groups(g0, last=False):
                        for s in range(2):
                            if not (last and s == 1):
                                queries(g0 + (s + 1))
                            turn(g0 + s)
                    groups(At(0))
                    with pe.Fori(1, NG // 2 - 1) as i:
                        groups(At(0, 2, i))
                    groups(At(NG - 2), True)

                @blk.scalar
                def _(act):
                    act.wait_ge(c_t, 1)
                    act.wait_ge(q_zero, 2)
                    kg = bank[6][:, 0:3 * W0].rearrange("p (t e) -> p t e", t=3)
                    act.activation(krg[:, 0:2, :], kg[:, 0:2, :], ACT.Copy).then_inc(c_ev, 1)
                    act.activation(krg[0:N_S, 2, :], kg[0:N_S, 2, :], ACT.Copy).then_inc(c_ev, 1)
                    act.wait_ge(c_ev, 2)
                    act.activation(gate_tok[:], krg[:, :, ROPE:], ACT.Copy).then_inc(c_ev, 1)
                    for t, (t0, n) in enumerate(TILES):
                        act.wait_ge(c_t, t + 2)
                        act.activation(c_tok[0:n, t, :], bank[3 + t][0:n, :], ACT.Copy).then_inc(c_ev, 1)

                    def out(g):
                        need(act, q_t, g.of(4, -4))
                        act.wait_ge(q_mm, g.of(1, 1))
                        for t, (t0, n) in enumerate(TILES):
                            act.activation(q_tok[0:n, g.mod(2), t].rearrange("p a e -> p (a e)"), bank[3 * g.mod(2) + t][0:n, 0:GW],
                                           ACT.Copy).then_inc(q_ev, 1)

                    def squares(g):
                        act.wait_ge(q_rot, g.of(2, 2))
                        need(act, q_ss, g.of())
                        act.activation(sqq[:], q_tok[:, g.mod(2)], ACT.Square).then_inc(q_sq, 1)
                        act.wait_ge(q_ss, g.of(1, 1))
                        act.activation(rq[:, g.mod(2), :], rq[:, g.mod(2), :], ACT.Sqrt, scale=1.0 / BQK, bias=eps).then_inc(q_rt, 1)

                    def turned(g):
                        for a in range(2):
                            act.wait_ge(q_t, g.of(4, 2 * a + 1))
                            act.activation(qT[:, bass.ds(g.of(2, a), 1), :].rearrange("p o t -> p (o t)"), bank[6][:, 0:T],
                                           ACT.Copy, scale=gq[:, 0:1]).then_inc(q_tev, 1)
                            act.wait_ge(q_t, g.of(4, 2 * a + 2))
                            act.activation(qrT[:, bass.ds(g.of(2, a), 1), :].rearrange("p o t -> p (o t)"), bank[7][0:ROPE, 0:T],
                                           ACT.Copy, scale=gq[0:ROPE, 1:2]).then_inc(q_tev, 1)
                    out(At(0))
                    act.wait_ge(q_zero, 4)

                    def groups(g0, last=False):
                        for s in range(2):
                            squares(g0 + s)
                            if not (last and s == 1):
                                out(g0 + (s + 1))
                            turned(g0 + s)
                    groups(At(0))
                    with act.Fori(1, NG // 2 - 1) as i:
                        groups(At(0, 2, i))
                    groups(At(NG - 2), True)

                @blk.vector
                def _(dve):
                    dve.memset(krg[:], 0.0).then_inc(q_zero, 1)
                    dve.memset(q_tok[:], 0.0).then_inc(q_zero, 1)
                    dve.scalar_tensor_tensor(gq[:, 0:1], vec[:, G_NQ:G_NQ + 1], SCALE, vec[:, G_NK:G_NK + 1], ALU.mult, ALU.mult).then_inc(q_zero, 1)
                    dve.scalar_tensor_tensor(gq[:, 1:2], vec[:, G_RQ:G_RQ + 1], SCALE, vec[:, G_RK:G_RK + 1], ALU.mult, ALU.mult).then_inc(q_zero, 1)
                    dve.wait_ge(c_ev, 2)
                    k1, k2 = krg[:, :, 0:h2], krg[:, :, h2:ROPE]
                    for j, (x, w) in enumerate(((k1, cos), (k2, sin), (k2, cos), (k1, sin))):
                        dve.tensor_tensor(rot[:, j, :, 0, :], x, w, ALU.mult).then_inc(c_rot, 1)
                    dve.wait_ge(c_rot, 4)
                    dve.tensor_tensor(krr[:, :, 0:h2], rot[:, 0, :, 0, :], rot[:, 1, :, 0, :], ALU.subtract).then_inc(q_dif, 1)
                    dve.tensor_tensor(krr[:, :, h2:], rot[:, 2, :, 0, :], rot[:, 3, :, 0, :], ALU.add).then_inc(q_dif, 1)
                    dve.wait_ge(q_dif, 2)

                    cb, sb_ = (x.unsqueeze(2).broadcast_to([P, 3, 2, h2]) for x in (cos, sin))

                    def rotate(g):
                        dve.wait_ge(q_ev, g.of(3, 3))
                        need(dve, q_rot, g.of(2))
                        x1, x2 = q_tok[:, g.mod(2), :, :, NOPE:NOPE + h2], q_tok[:, g.mod(2), :, :, NOPE + h2:]
                        for j, (x, w) in enumerate(((x1, cb), (x2, sb_), (x2, cb), (x1, sb_))):
                            dve.tensor_tensor(rot[:, j], x, w, ALU.mult).then_inc(q_m4, 1)
                        dve.wait_ge(q_m4, g.of(4, 4))
                        dve.tensor_tensor(x1, rot[:, 0], rot[:, 1], ALU.subtract).then_inc(q_rot, 1)
                        dve.tensor_tensor(x2, rot[:, 2], rot[:, 3], ALU.add).then_inc(q_rot, 1)

                    def scale(g):
                        dve.wait_ge(q_sq, g.of(1, 1))
                        dve.tensor_reduce(rq[:, g.mod(2), :].rearrange("p (t a) -> p t a", a=2), sqq[:], AX.X, ALU.add).then_inc(q_ss, 1)
                        dve.wait_ge(q_rt, g.of(1, 1))
                        dve.reciprocal(rq[:, g.mod(2), :], rq[:, g.mod(2), :]).then_inc(q_rc, 1)
                        dve.wait_ge(q_rc, g.of(1, 1))
                        q = q_tok[:, g.mod(2)].rearrange("p t a e -> p (t a) e")
                        dve.tensor_tensor(q, q, rq[:, g.mod(2), :].unsqueeze(2).broadcast_to([P, 6, BQK]), ALU.mult).then_inc(q_nrm, 1)

                    def groups(g0):
                        for s in range(2):
                            rotate(g0 + s)
                            scale(g0 + s)
                    groups(At(0))
                    with dve.Fori(1, NG // 2) as i:
                        groups(At(0, 2, i))

        with ExitStack() as ph:
            k_tok = sb(ph, "k_tok", [P, 2, 4 * NOPE])
            sqk = sb(ph, "sqk", [P, 2, 4 * NOPE])
            krh = sb(ph, "krh", [P, 2, 4, ROPE])
            rkp = sb(ph, "rkp", [P, 2, 4])
            sqr2 = sb(ph, "sqr2", [P, 3, ROPE])
            ssr2 = sb(ph, "ssr2", [P, 3])
            ukT = sb(ph, "ukT", [P, 2, KVL])
            (k_mm, k_ev, k_sq, k_ss, k_ad, k_rt, k_rc, k_sc, k_sr, k_t, k_tev, k_r2, k_s2) = (
                sem("k_" + x) for x in ("mm", "ev", "sq", "ss", "ad", "rt", "rc", "sc", "sr", "t", "tev", "r2", "s2"))
            u_t, u_ev, u_q, u_qev = (sem("u_" + x) for x in ("t", "ev", "q", "qev"))
            UNITS = [(t, g) for t in range(3) for g in range(4)]
            NTU = 8
            with nc.Block() as blk:
                @blk.tensor
                def _(pe):
                    pe.wait_ge(uk_in, 32 * LC)

                    def keys(u):
                        t, g = UNITS[u]
                        t0, n = TILES[t]
                        need(pe, k_ev, u - 1)
                        for k in range(LC):
                            mm = pe.matmul(bank[u % 2][0:n, :], ckvT[:, k, t0:t0 + n], stage[:, k, g * 512:(g + 1) * 512],
                                           start=k == 0, stop=k == LC - 1)
                        mm.then_inc(k_mm, 1)

                    def turn(u):
                        need(pe, k_tev, 2 * u)
                        pe.wait_ge(k_sc, u + 1)
                        for a in range(4):
                            tr = pe.transpose(bank[2][:, a * P:(a + 1) * P], k_tok[:, u % 2, a * P:(a + 1) * P], ident)
                        tr.then_inc(k_t, 1)
                        pe.wait_ge(k_sr, u + 1)
                        for a in range(4):
                            tr = pe.transpose(bank[3][0:ROPE, a * P:(a + 1) * P], krh[:, u % 2, a, :], ident)
                        tr.then_inc(k_t, 1)

                    def flip(h):
                        need(pe, u_ev, h - 1)
                        for k in range(LC):
                            tr = pe.transpose(bank[4 + h % 2][:, k * P:(k + 1) * P], stage[:, k, h * P:(h + 1) * P], ident)
                        tr.then_inc(u_t, 1)

                    def absorb(h):
                        pe.wait_ge(u_ev, h + 1)
                        need(pe, u_qev, h - 1)
                        for k in range(LC):
                            mm = pe.matmul(bank[6 + h % 2][:, k * N_S:(k + 1) * N_S], ukT[:, h % 2, k * P:(k + 1) * P], qT[:, h, S_P:],
                                           start=True, stop=True)
                        mm.then_inc(u_q, 1)
                    keys(0)
                    flip(0)
                    for u in range(12):
                        if u < 11:
                            keys(u + 1)
                        flip(u + 1)
                        absorb(u)
                        if u < NTU:
                            turn(u)
                    for h in range(12, BH):
                        if h + 1 < BH:
                            flip(h + 1)
                        absorb(h)

                @blk.scalar
                def _(act):
                    for t in range(3):
                        act.activation(sqr2[:, t, :], krr[:, t, :], ACT.Square, accum_out=ssr2[:, t:t + 1]).then_inc(k_r2, 1)

                    def keys(u):
                        t, g = UNITS[u]
                        n = TILES[t][1]
                        act.wait_ge(k_mm, u + 1)
                        if u >= 2:
                            need(act, k_t, min(2 * (u - 1), 2 * NTU))
                            act.wait_ge(k_ss, u - 1)
                        act.activation(k_tok[0:n, u % 2, :], bank[u % 2][0:n, :], ACT.Copy)
                        act.activation(sqk[0:n, u % 2, :], bank[u % 2][0:n, :], ACT.Square).then_inc(k_ev, 1)

                    def root(u):
                        n = TILES[UNITS[u][0]][1]
                        act.wait_ge(k_ad, u + 1)
                        act.activation(rkp[0:n, u % 2, :], rkp[0:n, u % 2, :], ACT.Sqrt, scale=1.0 / BQK, bias=eps[0:n]).then_inc(k_rt, 1)

                    def turned(u):
                        t, g = UNITS[u]
                        act.wait_ge(k_t, 2 * u + 1)
                        act.activation(KT[:, 4 * g:4 * g + 4, t * P:(t + 1) * P], bank[2][:].rearrange("p (a s) -> p a s", a=4),
                                       ACT.Copy).then_inc(k_tev, 1)
                        act.wait_ge(k_t, 2 * u + 2)
                        act.activation(krT[:, 4 * g:4 * g + 4, t * P:(t + 1) * P], bank[3][0:ROPE].rearrange("p (a s) -> p a s", a=4),
                                       ACT.Copy).then_inc(k_tev, 1)

                    def flipped(h):
                        act.wait_ge(u_t, h + 1)
                        need(act, u_q, h - 1)
                        act.activation(ukT[:, h % 2, :], bank[4 + h % 2][:], ACT.Copy).then_inc(u_ev, 1)
                    keys(0)
                    for u in range(12):
                        flipped(u)
                        if u < 11:
                            keys(u + 1)
                        root(u)
                        if u < NTU:
                            turned(u)
                    for h in range(12, BH):
                        flipped(h)

                @blk.vector
                def _(dve):
                    dve.wait_ge(k_r2, 3)

                    def absorbed(h):
                        dve.wait_ge(u_q, h + 1)
                        dve.tensor_copy(qlat[:, :, :, h, :], bank[6 + h % 2][:, 0:LC * N_S].rearrange("p (k b s) -> p k b s", k=LC, b=NB)).then_inc(u_qev, 1)
                    for u, (t, g) in enumerate(UNITS):
                        n = TILES[t][1]
                        dve.wait_ge(k_ev, u + 1)
                        need(dve, k_rc, u - 1)
                        dve.tensor_reduce(rkp[0:n, u % 2, :], sqk[0:n, u % 2, :].rearrange("p (a d) -> p a d", a=4), AX.X, ALU.add).then_inc(k_ss, 1)
                        dve.wait_ge(k_ss, u + 1)
                        dve.tensor_scalar(rkp[0:n, u % 2, :], rkp[0:n, u % 2, :], ssr2[0:n, t:t + 1], None, ALU.add).then_inc(k_ad, 1)
                        dve.wait_ge(k_rt, u + 1)
                        if t == 2:
                            dve.reciprocal(rk_new[0:n, 4 * g:4 * g + 4], rkp[0:n, u % 2, :]).then_inc(k_rc, 1)
                        else:
                            dve.reciprocal(rkp[:, u % 2, :], rkp[:, u % 2, :]).then_inc(k_rc, 1)
                            dve.wait_ge(k_rc, u + 1)
                            kk = k_tok[:, u % 2, :].rearrange("p (a d) -> p a d", a=4)
                            dve.tensor_tensor(kk, kk, rkp[:, u % 2, :].unsqueeze(2).broadcast_to([P, 4, NOPE]), ALU.mult).then_inc(k_sc, 1)
                            need(dve, k_t, 2 * (u - 1))
                            dve.tensor_tensor(krh[:, u % 2], krr[:, t, :].unsqueeze(1).broadcast_to([P, 4, ROPE]),
                                              rkp[:, u % 2, :].unsqueeze(2).broadcast_to([P, 4, ROPE]), ALU.mult).then_inc(k_sr, 1)
                        absorbed(u)
                    for h in range(12, BH):
                        absorbed(h)
        with ExitStack() as ph:
            v_tok = sb(ph, "v_tok", [P, 2, 2, BV])
            qh = sb(ph, "qh", [P, 2, S_P])
            qrh = sb(ph, "qrh", [ROPE, 2, S_P])
            sm = sb(ph, "sm_p", [P, 2, 3 * P])
            mx = sb(ph, "mx_p", [P, 2, 2])
            sums = sb(ph, "sums_p", [P, 2, 2])
            pT = sb(ph, "pT", [P, 2, 3 * P])
            ho = sb(ph, "ho", [P, 2, S_P])
            uv_in = sem("uv_in")
            (e_q, e_v, e_vev, e_s, e_sm, e_mx, e_ex, e_rc, e_nm, e_t, e_tev, e_o, e_oev) = (
                sem("e_" + x) for x in ("q", "v", "vev", "s", "sm", "mx", "ex", "rc", "nm", "t", "tev", "o", "oev"))
            e_st = [sem("e_st0"), sem("e_st1")]
            PARTS = ((0, 128), (128, 384))
            seen = C("seen")
            with nc.Block() as blk:
                @blk.sync
                def _(sp):
                    for k in range(LC):
                        sp.dma_start(stage[:, k, :], A["w_uv"][0, k * P:(k + 1) * P].rearrange("c h d -> c (h d)")).then_inc(uv_in, 16)

                    def out(h):
                        sp.wait_ge(e_oev, h.of(1, 1))
                        sp.dma_start(hb_dram[:, bass.ds(h.of(), 1), 0:S_P].rearrange("p o t -> p (o t)"), ho[:, h.mod(2), :]).then_inc(e_st[h.mod(2)], 16)
                    with sp.Fori(0, BH // 2) as i:
                        for s in range(2):
                            out(At(s, 2, i))
                    for s in range(2):
                        sp.wait_ge(e_st[s], 8 * BH)

                @blk.tensor
                def _(pe):
                    def scores(h):
                        a = h.mod(2)
                        need(pe, e_vev, h.of(1, -1))
                        for t in range(2):
                            for k in range(LC):
                                mm = pe.matmul(bank[a][:, t * BV:(t + 1) * BV], ckvT[:, k, t * P:(t + 1) * P],
                                               stage[:, k, bass.ds(h.of() * BV, BV)], start=k == 0, stop=k == LC - 1)
                        mm.then_inc(e_v, 1)
                        pe.wait_ge(e_q, h.of(2, 2))
                        need(pe, e_sm, h.of(1, -1))
                        for t, (c0, c1) in enumerate(PARTS):
                            keys = slice(0, c1 - c0)
                            pe.matmul(bank[2 + a][:, c0:c1], qh[:, a, t * P:(t + 1) * P],
                                      KT[:, bass.ds(h.of(), 1), keys].rearrange("p o s -> p (o s)"), start=True, stop=False)
                            mm = pe.matmul(bank[2 + a][:, c0:c1], qrh[:, a, t * P:(t + 1) * P],
                                           krT[:, bass.ds(h.of(), 1), keys].rearrange("p o s -> p (o s)"), start=False, stop=True)
                        mm.then_inc(e_s, 1)

                    def values(h):
                        a = h.mod(2)
                        pe.wait_ge(e_nm, h.of(2, 2))
                        need(pe, e_tev, h.of(1, -1))
                        for src, dst in ((0, 0), (1, 1), (2, 2)):
                            tr = pe.transpose(bank[4 + a][:, dst * P:(dst + 1) * P], sm[:, a, src * P:(src + 1) * P], ident)
                        tr.then_inc(e_t, 1)
                        pe.wait_ge(e_tev, h.of(1, 1))
                        pe.wait_ge(e_vev, h.of(1, 1))
                        need(pe, e_oev, h.of(1, -1))
                        pe.matmul(bank[6 + a][:, 0:S_P], v_tok[:, a, 0, :], pT[:, a, 0:S_P], start=True, stop=False)
                        pe.matmul(bank[6 + a][:, P:S_P], v_tok[:, a, 1, :], pT[:, a, S_P:], start=False, stop=True).then_inc(e_o, 1)
                    pe.wait_ge(uv_in, 16 * LC)
                    scores(At(0))

                    def heads_(h0, last=False):
                        for s in range(2):
                            if not (last and s == 1):
                                scores(h0 + (s + 1))
                            values(h0 + s)
                    heads_(At(0))
                    with pe.Fori(1, BH // 2 - 1) as i:
                        heads_(At(0, 2, i))
                    heads_(At(BH - 2), True)

                @blk.scalar
                def _(act):
                    def value(h):
                        a = h.mod(2)
                        act.wait_ge(e_v, h.of(1, 1))
                        need(act, e_o, h.of(1, -1))
                        act.activation(v_tok[:, a].rearrange("p t d -> p (t d)"), bank[a][:, 0:2 * BV], ACT.Copy).then_inc(e_vev, 1)

                    def exps(h):
                        a = h.mod(2)
                        act.wait_ge(e_mx, h.of(2, 2))
                        for t, (c0, c1) in enumerate(PARTS):
                            act.activation(sm[:, a, c0:c1], sm[:, a, c0:c1], ACT.Exp, bias=mx[:, a, t:t + 1], accum_out=sums[:, a, t:t + 1]).then_inc(e_ex, 1)

                    def turned(h):
                        a = h.mod(2)
                        act.wait_ge(e_t, h.of(1, 1))
                        need(act, e_o, h.of(1, -1))
                        act.activation(pT[:, a, :], bank[4 + a][:, 0:3 * P], ACT.Copy).then_inc(e_tev, 1)
                        act.wait_ge(e_o, h.of(1, 1))
                        need(act, e_st[a], h.div(2, 0, 16))
                        act.activation(ho[:, a, :], bank[6 + a][:, 0:S_P], ACT.Copy).then_inc(e_oev, 1)
                    value(At(0))

                    def heads_(h0, last=False):
                        for s in range(2):
                            exps(h0 + s)
                            if not (last and s == 1):
                                value(h0 + (s + 1))
                            turned(h0 + s)
                    heads_(At(0))
                    with act.Fori(1, BH // 2 - 1) as i:
                        heads_(At(0, 2, i))
                    heads_(At(BH - 2), True)

                @blk.vector
                def _(dve):
                    def place(h):
                        a = h.mod(2)
                        need(dve, e_s, h.of(1, -1))
                        dve.tensor_copy(qh[:, a, :], qT[:, bass.ds(h.of(), 1), 0:S_P].rearrange("p o t -> p (o t)")).then_inc(e_q, 1)
                        dve.tensor_copy(qrh[:, a, :], qrT[:, bass.ds(h.of(), 1), 0:S_P].rearrange("p o t -> p (o t)")).then_inc(e_q, 1)

                    def soft(h):
                        a = h.mod(2)
                        dve.wait_ge(e_s, h.of(1, 1))
                        need(dve, e_t, h.of(1, -1))
                        dve.tensor_tensor(sm[:, a, :], bank[2 + a][:, 0:3 * P], seen, ALU.add).then_inc(e_sm, 1)
                        dve.wait_ge(e_sm, h.of(1, 1))
                        for t, (c0, c1) in enumerate(PARTS):
                            dve.tensor_reduce(mx[:, a, t:t + 1], sm[:, a, c0:c1], AX.X, ALU.max, negate=True).then_inc(e_mx, 1)

                    def norm_(h):
                        a = h.mod(2)
                        dve.wait_ge(e_ex, h.of(2, 2))
                        dve.reciprocal(sums[:, a, :], sums[:, a, :]).then_inc(e_rc, 1)
                        dve.wait_ge(e_rc, h.of(1, 1))
                        for t, (c0, c1) in enumerate(PARTS):
                            dve.tensor_scalar(sm[:, a, c0:c1], sm[:, a, c0:c1], sums[:, a, t:t + 1], None, ALU.mult).then_inc(e_nm, 1)
                    place(At(0))
                    place(At(1))
                    soft(At(0))

                    def heads_(h0, last=False):
                        for s in range(2):
                            norm_(h0 + s)
                            if not last:
                                place(h0 + (s + 2))
                            if not (last and s == 1):
                                soft(h0 + (s + 1))
                    heads_(At(0))
                    with dve.Fori(1, BH // 2 - 1) as i:
                        heads_(At(0, 2, i))
                    heads_(At(BH - 2), True)
        heads.close()

        with ExitStack() as ph:
            NJ = NPG + 1
            HQ = BH * S_S
            latf = sb(ph, "latf", [P, 2, NPG, KVL + ROPE])
            latT = sb(ph, "latT", [P, 2, KVL])
            rT = sb(ph, "rT", [ROPE, 2, P])
            sc = sb(ph, "sc_s", [P, 2, NJ, HQ])
            mxp = sb(ph, "mxp", [P, 2, P])
            mxc = sb(ph, "mxc", [HQ, 2])
            mxw = sb(ph, "mxw", [HQ, 2, P])
            rs = sb(ph, "rs", [P, 2, HQ])
            olat = sb(ph, "olat", [P, LC, BH, N_S])
            hs = sb(ph, "hs", [P, BH, N_S])
            krrT = sb(ph, "krrT", [ROPE, P])
            cnT = sb(ph, "cnT", [P, LC, P])
            f_in = [[sem(f"f_in{b}_{j}") for j in range(2)] for b in range(2)]
            (f_t, f_ev, f_s, f_sev, f_mxp, f_mt, f_mc, f_mw, f_mb, f_sub, f_ex, f_o, f_rs, f_oev, f_neg, f_h, f_hev) = (
                sem("f_" + x) for x in ("t", "ev", "s", "sev", "mxp", "mt", "mc", "mw", "mb", "sub", "ex", "o", "rs", "oev", "neg", "h", "hev"))
            f_zero = sem("f_zero")
            new_seen = C("new_seen").rearrange("p (b s) -> p b s", b=NB)
            HALF = NPG // 2
            with nc.Block() as blk:
                @blk.sync
                def _(sp):
                    def batch(b):
                        need(sp, f_o, b.of(1, -1))
                        for j in range(NPG):
                            v = sp.value_load(page[0:1, bass.ds(b.of(NPG, j), 1)], min_val=0, max_val=NPOOL - 1)
                            dst = latf[:, b.mod(2), j]
                            sp.dma_start(dst[:, 0:KVL], lat_v[bass.ds(v, 1)].rearrange("o p c -> (o p) c")).then_inc(f_in[b.mod(2)][j // HALF], 16)
                            sp.dma_start(dst[:, KVL:], kr_v[bass.ds(v, 1)].rearrange("o p c -> (o p) c")).then_inc(f_in[b.mod(2)][j // HALF], 16)
                    batch(At(0))
                    batch(At(1))
                    with sp.Fori(1, NB // 2) as i:
                        batch(At(0, 2, i))
                        batch(At(1, 2, i))
                    sp.wait_ge(f_hev, BH)
                    sp.dma_start(hb_dram[:, :, S_P:], hs[:]).then_inc(e_st[0], 16)
                    sp.wait_ge(e_st[0], 8 * BH + 16)

                @blk.tensor
                def _(pe):
                    def turn(b, j):
                        n = b.of(NPG, j)
                        if j % HALF == 0:
                            pe.wait_ge(f_in[b.mod(2)][j // HALF], b.div(2, 1, 32 * HALF))
                        need(pe, f_ev, b.of(2 * NPG, 2 * (j - 1)))
                        for k in range(LC):
                            pe.transpose(bank[j % 2][:, k * P:(k + 1) * P], latf[:, b.mod(2), j, k * P:(k + 1) * P], ident)
                        pe.transpose(bank[6 + j % 2][0:ROPE, 0:P], latf[:, b.mod(2), j, KVL:], ident).then_inc(f_t, 1)

                    def score(b, j):
                        a = b.mod(2)
                        pe.wait_ge(f_ev, b.of(2 * NPG, 2 * j + 2))
                        need(pe, f_sev, b.of(NJ, max(j - 1, 0)))
                        ps = bank[2 + j % 2][:, 0:HQ]
                        for k in range(LC):
                            pe.matmul(ps, latT[:, j % 2, k * P:(k + 1) * P], qlat[:, k, bass.ds(b.of(), 1)].rearrange("p o h s -> p (o h s)"),
                                      start=k == 0, stop=False)
                        pe.matmul(ps, rT[:, j % 2, :], qrT[:, :, bass.ds(b.of(S_S, S_P), S_S)], start=False, stop=True).then_inc(f_s, 1)

                    def score_new(b):
                        need(pe, f_sev, b.of(NJ, NPG - 1))
                        ps = bank[2][:, 0:HQ]
                        for k in range(LC):
                            pe.matmul(ps, cnT[:, k, :], qlat[:, k, bass.ds(b.of(), 1)].rearrange("p o h s -> p (o h s)"), start=k == 0, stop=False)
                        pe.matmul(ps, krrT[:], qrT[:, :, bass.ds(b.of(S_S, S_P), S_S)], start=False, stop=True).then_inc(f_s, 1)

                    def batch(b):
                        turn(b, 0)
                        for j in range(NPG):
                            if j + 1 < NPG:
                                turn(b, j + 1)
                            score(b, j)
                        score_new(b)

                    def maxima(b):
                        a = b.mod(2)
                        pe.wait_ge(f_mxp, b.of(1, 1))
                        pe.transpose(bank[4][:, 0:P], mxp[:, a, :], ident).then_inc(f_mt, 1)
                        pe.wait_ge(f_mw, b.of(1, 1))
                        pe.matmul(bank[4][:, P:P + HQ], mxw[:, a, :], ident[0:HQ, 0:HQ], start=True, stop=True).then_inc(f_mb, 1)

                    def values(b):
                        a = b.mod(2)
                        pe.wait_ge(f_ex, b.of(1, 1))
                        need(pe, f_oev, b.of(1))
                        for k in range(LC + 1):
                            for j in range(NJ):
                                n = P if j < NPG else N_S
                                w = ones[0:n, :] if k == LC else latf[:, a, j, k * P:(k + 1) * P] if j < NPG else c_tok[0:N_S, 2, k * P:(k + 1) * P]
                                mm = pe.matmul(bank[5][:, k * HQ:(k + 1) * HQ], w, sc[0:n, a, j, :], start=j == 0, stop=j == NJ - 1)
                        mm.then_inc(f_o, 1)
                    pe.transpose(bank[7][0:ROPE, 0:N_S], krr[0:N_S, 2, :], ident[0:N_S, 0:N_S]).then_inc(f_t, 1)
                    pe.wait_ge(f_neg, 2)
                    batch(At(0))

                    def pair(b0, last=False):
                        for s in range(2):
                            maxima(b0 + s)
                            if not (last and s == 1):
                                batch(b0 + (s + 1))
                            values(b0 + s)
                    pair(At(0))
                    with pe.Fori(1, NB // 2 - 1) as i:
                        pair(At(0, 2, i))
                    pair(At(NB - 2), True)
                    pe.wait_ge(f_oev, NB)
                    for h in range(BH):
                        need(pe, f_hev, h - 1)
                        for k in range(LC):
                            mm = pe.matmul(bank[h % 2][:, 0:N_S], stage[:, k, h * BV:(h + 1) * BV], olat[:, k, h, :], start=k == 0, stop=k == LC - 1)
                        mm.then_inc(f_h, 1)

                @blk.scalar
                def _(act):
                    def turned(b, j):
                        act.wait_ge(f_t, b.of(NPG, j + 2))
                        need(act, f_s, b.of(NJ, j - 1))
                        act.activation(latT[:, j % 2, :], bank[j % 2][:], ACT.Copy).then_inc(f_ev, 1)
                        act.activation(rT[:, j % 2, :], bank[6 + j % 2][0:ROPE, 0:P], ACT.Copy).then_inc(f_ev, 1)
                    act.wait_ge(f_t, 1)
                    act.wait_ge(f_zero, 5)
                    act.activation(krrT[:, 0:N_S], bank[7][0:ROPE, 0:N_S], ACT.Copy).then_inc(f_neg, 1)

                    def batch(b):
                        for j in range(NPG):
                            turned(b, j)

                    def exps(b):
                        act.wait_ge(f_sub, b.of(1, 1))
                        act.activation(sc[:, b.mod(2)], sc[:, b.mod(2)], ACT.Exp).then_inc(f_ex, 1)
                    batch(At(0))

                    def pair(b0, last=False):
                        for s in range(2):
                            exps(b0 + s)
                            if not (last and s == 1):
                                batch(b0 + (s + 1))
                    pair(At(0))
                    with act.Fori(1, NB // 2 - 1) as i:
                        pair(At(0, 2, i))
                    pair(At(NB - 2), True)
                    for h in range(BH):
                        act.wait_ge(f_h, h + 1)
                        act.activation(hs[:, h, :], bank[h % 2][:, 0:N_S], ACT.Copy).then_inc(f_hev, 1)

                @blk.vector
                def _(dve):
                    for a in range(2):
                        dve.memset(sc[:, a, NPG, :], NEG).then_inc(f_zero, 1)
                    dve.memset(mxp[:], 0.0).then_inc(f_zero, 1)
                    dve.memset(krrT[:], 0.0).then_inc(f_zero, 1)
                    dve.memset(cnT[:], 0.0).then_inc(f_zero, 1)
                    dve.wait_ge(f_zero, 5)
                    dve.tensor_copy(cnT[:, :, 0:N_S], ckvT[:, :, S_P:]).then_inc(f_neg, 1)

                    def batch(b):
                        a = b.mod(2)
                        need(dve, f_o, b.of(1, -1))
                        for j in range(NPG):
                            dve.wait_ge(f_s, b.of(NJ, j + 1))
                            dve.tensor_tensor(sc[:, a, j, :].rearrange("p (h s) -> p h s", s=S_S),
                                              bank[2 + j % 2][:, 0:HQ].rearrange("p (h s) -> p h s", s=S_S),
                                              rk[:, bass.ds(b.of(NPG, j), 1), :].rearrange("p o h -> p (o h)").unsqueeze(2).broadcast_to([P, BH, S_S]),
                                              ALU.mult).then_inc(f_sev, 1)
                        dve.wait_ge(f_s, b.of(NJ, NJ))
                        new = sc[0:N_S, a, NPG, :].rearrange("p (h s) -> p h s", s=S_S)
                        dve.tensor_tensor(new, bank[2][0:N_S, 0:HQ].rearrange("p (h s) -> p h s", s=S_S),
                                          rk_new[0:N_S].unsqueeze(2).broadcast_to([N_S, BH, S_S]), ALU.mult).then_inc(f_sev, 1)
                        dve.wait_ge(f_sev, b.of(NJ, NJ))
                        dve.tensor_tensor(new, new, new_seen[:, bass.ds(b.of(), 1), :].broadcast_to([N_S, BH, S_S]), ALU.add).then_inc(f_mc, 1)
                        dve.wait_ge(f_mc, b.of(2, 1))
                        dve.tensor_reduce(mxp[:, a, 0:HQ], sc[:, a].rearrange("p j q -> p q j"), AX.X, ALU.max).then_inc(f_mxp, 1)

                    def maxima(b):
                        a = b.mod(2)
                        dve.wait_ge(f_mt, b.of(1, 1))
                        dve.tensor_reduce(mxc[:, a:a + 1], bank[4][0:HQ, 0:P], AX.X, ALU.max).then_inc(f_mc, 1)
                        dve.wait_ge(f_mc, b.of(2, 2))
                        dve.tensor_copy(mxw[:, a, :], mxc[:, a:a + 1].broadcast_to([HQ, P])).then_inc(f_mw, 1)
                        dve.wait_ge(f_mb, b.of(1, 1))
                        dve.tensor_tensor(sc[:, a], sc[:, a], bank[4][:, P:P + HQ].unsqueeze(1).broadcast_to([P, NJ, HQ]), ALU.subtract).then_inc(f_sub, 1)

                    def out(b):
                        a = b.mod(2)
                        dve.wait_ge(f_o, b.of(1, 1))
                        dve.reciprocal(rs[:, a, :], bank[5][:, LC * HQ:(LC + 1) * HQ]).then_inc(f_rs, 1)
                        dve.wait_ge(f_rs, b.of(1, 1))
                        for k in range(LC):
                            ins = dve.tensor_tensor(olat[:, k, :, bass.ds(b.of(S_S), S_S)], bank[5][:, k * HQ:(k + 1) * HQ].rearrange("p (h s) -> p h s", s=S_S),
                                                    rs[:, a, :].rearrange("p (h s) -> p h s", s=S_S), ALU.mult)
                        ins.then_inc(f_oev, 1)
                    batch(At(0))

                    def pair(b0, last=False):
                        for s in range(2):
                            maxima(b0 + s)
                            if not (last and s == 1):
                                batch(b0 + (s + 1))
                            out(b0 + s)
                    pair(At(0))
                    with dve.Fori(1, NB // 2 - 1) as i:
                        pair(At(0, 2, i))
                    pair(At(NB - 2), True)
        kept.close()
        recycle()
        def head_load(sp, h, m):
            base, mul = ((O_Q, P), (O_K, P), (O_V, DV), (O_V + P, DV), (O_O, DV), (O_O + P, DV))[m]
            w_load(sp, At(N0 + 6 * h.c + m, 6 * h.step, h.i), w_in_v, h.of(mul, base))

        def branch_load(sp, c, m, n0, view, gate):
            w_load(sp, At(n0 + 2 * c.c + m, 2 * c.step, c.i), w_in_v if m % 2 else view, c.of(P, m // 2 * P + (gate if m % 2 else 0)))

        haH = sb(ctx, "haH", [P, KC, T], F32R)
        haL = sb(ctx, "haL", [P, KC, T], F32R)
        DVE_ = DV + 1
        ws["hi"] = sb(ctx, "w_hi_b", [P, 2, KC * P], F32R)
        ws["lo"] = sb(ctx, "w_lo_b", [P, 2, KC * P], F32R)
        hd = ctx.enter_context(ExitStack())
        ga = sb(hd, "ga", [P, 3, AH])
        gem = sb(hd, "gem", [P, 3, AH])
        gwk = sb(hd, "gwk", [P, 3, AH])
        gws = sb(hd, "gws", [N_S, AH])
        neg_MT = sb(hd, "neg_MT", [AH, T])
        decb = sb(hd, "decb", [P, NB, AH])
        nT = sb(hd, "nT", [P, NB, AH])
        n_all = sb(hd, "n_all", [P, AH + NB * AH])
        with ExitStack() as ph:
            gb = sb(ph, "gb", [P, 2 * AH])
            g3 = sb(ph, "g3", [P, 3, 2 * AH])
            li = sb(ph, "li", [P, 3, AH])
            nlf = sb(ph, "nlf", [P, 3, AH])
            nb_ = sb(ph, "nb_", [P, 5, AH])
            aT = sb(ph, "aT", [AH, T])
            M = sb(ph, "M", [P, 3, AH])
            Me = sb(ph, "Me", [P, 2, AH])
            t0_ = sb(ph, "t0_", [P, 4, 3 * P])
            m0s = sb(ph, "m0s", [N_S, AH])
            dif = sb(ph, "dif", [P, 8, AH])
            decm = sb(ph, "decm", [N_S, NB, AH])
            m_out = sb(ph, "m_out", [P, 2, AH])
            n_rows = sb(ph, "n_rows", [NB * AH, P])
            g_in, g_pe, g_act, g_cp, g_a, g_row, g_red = (sem("g_" + x) for x in ("in", "pe", "act", "cp", "a", "row", "red"))
            vo = dve_own
            with nc.Block() as blk:
                @blk.sync
                def _(sp):
                    sp.dma_start(gb[:], A["b_gates"].broadcast_to([P, 2 * AH])).then_inc(g_in, 16)
                    for s in range(S_S):
                        sp.dma_start(m0s[s:N_S:S_S, :], A["state_mlstm_m"][0]).then_inc(g_in, 16)
                    sp.dma_start(n_rows[:], A["state_mlstm_n"][0].rearrange("b h d -> (b h) d")).then_inc(g_in, 16)
                    for m in range(4):
                        head_load(sp, At(0), m)
                    sp.wait_ge(g_cp, 2)
                    store(sp, O["mlstm_m_p"][0], m_out[0:1, 0, :])
                    store(sp, O["mlstm_m_s"][0], m_out[0:N_S:S_S, 1, :])
                    all_stored(sp)

                @blk.scalar
                def _(act):
                    act.wait_ge(g_cp, 1)
                    act.activation(g3[:], g3[:], ACT.Tanh, scale=1.0 / CAP).then_inc(g_act, 1)
                    act.wait_ge(g_act, 1)
                    act.activation(nlf[:], g3[:, :, AH:], ACT.Exp, scale=-CAP).then_inc(g_act, 1)
                    act.wait_ge(g_act, 2)
                    act.activation(nlf[:], nlf[:], ACT.Ln, bias=ones[:, 0:1]).then_inc(g_act, 1)
                    act.activation(li[:], g3[:, :, 0:AH], ACT.Copy, scale=CAP).then_inc(g_act, 1)
                    act.wait_ge(g_cp, 2)
                    act.activation(dif[:], dif[:], ACT.Exp).then_inc(g_act, 1)
                    act.wait_ge(g_pe, 4)
                    act.activation(neg_MT[:], bank[2][0:AH, 0:T], ACT.Copy, scale=-1.0).then_inc(g_act, 1)

                @blk.tensor
                def _(pe):
                    pe.wait_ge(g_act, 3)
                    up, ups, same = C("upto"), C("upto_s"), C("same_s")
                    b0 = bank[0]
                    pe.matmul(b0[:, 0:AH], up, nlf[:, 0, :], start=True, stop=True)
                    pe.matmul(b0[:, AH:2 * AH], ones, nlf[:, 0, :], start=True, stop=False)
                    pe.matmul(b0[:, AH:2 * AH], up, nlf[:, 1, :], start=False, stop=True)
                    pe.matmul(b0[0:N_S, 2 * AH:3 * AH], ups, nlf[0:N_S, 2, :], start=True, stop=True)
                    pe.matmul(b0[:, 3 * AH:4 * AH], ones, nlf[:, 0, :], start=True, stop=False)
                    pe.matmul(b0[:, 3 * AH:4 * AH], ones, nlf[:, 1, :], start=False, stop=True)
                    pe.matmul(b0[0:N_S, 4 * AH:5 * AH], same, nlf[0:N_S, 2, :], start=True, stop=True).then_inc(g_pe, 1)
                    pe.wait_ge(g_in, 16 * 6)
                    pe.transpose(bank[3][:, 0:NB * AH], n_rows[:], ident[0:NB * AH, 0:NB * AH]).then_inc(g_pe, 1)
                    pe.wait_ge(g_a, 1)
                    for t, (q0, n) in enumerate(TILES):
                        tr = pe.transpose(bank[1][0:AH, q0:q0 + n], ga[0:n, t, :], ident[0:n, 0:n])
                    tr.then_inc(g_pe, 1)
                    pe.wait_ge(g_a, 2)
                    pick = C("pick").rearrange("p (h m) -> p h m", h=AH)
                    for h in range(AH):
                        if h >= 4:
                            pe.wait_ge(g_red, h - 3)
                        pe.matmul(bank[4 + h % 4][:, 0:T], pick[:, h, :], aT[:], start=True, stop=True).then_inc(g_row, 1)
                    pe.wait_ge(g_cp, 2)
                    for t, (q0, n) in enumerate(TILES):
                        tr = pe.transpose(bank[2][0:AH, q0:q0 + n], M[0:n, t, :], ident[0:n, 0:n])
                    tr.then_inc(g_pe, 1)
                    pe.wait_ge(g_a, 3)
                    pe.matmul(bank[1][:, 0:NB * AH], ones[0:N_S, :], decm[:].rearrange("p b h -> p (b h)"), start=True, stop=True).then_inc(g_pe, 1)

                @blk.vector
                def _(dve):
                    dve.memset(t0_[:], 0.0)
                    dve.memset(M[:], 0.0)
                    dve.memset(Me[:], 0.0)
                    dve.memset(nb_[:], 0.0)
                    vo.step(dve, dve.memset(ga[:], 0.0))
                    vo.step(dve, dve.memset(dif[:], 0.0))
                    dve.wait_ge(g_in, 16 * 6)
                    dve.tensor_tensor(g3[:], gate_tok[:], gb[:].unsqueeze(1).broadcast_to([P, 3, 2 * AH]), ALU.add).then_inc(g_cp, 1)
                    dve.wait_ge(g_pe, 1)
                    dve.wait_ge(g_act, 4)
                    dve.tensor_copy(nb_[:, 0:2, :], bank[0][:, 0:2 * AH].rearrange("p (t h) -> p t h", h=AH))
                    dve.tensor_copy(nb_[:, 3, :], bank[0][:, 3 * AH:4 * AH])
                    vo.step(dve, dve.tensor_copy(nb_[0:N_S, 2:5:2, :], bank[0][0:N_S, 2 * AH:].rearrange("p (t h) -> p t h", h=AH)[:, 0:3:2, :]))
                    dve.tensor_tensor(ga[:], li[:], nb_[:, 0:3, :], ALU.add).then_inc(g_a, 1)
                    dve.wait_ge(g_pe, 3)
                    dve.tensor_copy(nT[:].rearrange("p b h -> p (b h)"), bank[3][:, 0:NB * AH])
                    dve.tensor_copy(aT[:], bank[1][0:AH, 0:T]).then_inc(g_a, 1)
                    seen_, seen_s, same_neg = C("seen"), C("seen_s"), C("same_neg")
                    for h in range(AH):
                        dve.wait_ge(g_row, h + 1)
                        row = bank[4 + h % 4]
                        dve.tensor_tensor(t0_[:, 0, 0:P], row[:, 0:P], seen_[:, 0:P], ALU.add)
                        dve.tensor_tensor(t0_[:, 1, 0:S_P], row[:, 0:S_P], seen_[:, P:], ALU.add)
                        dve.tensor_tensor(t0_[0:N_S, 2, 0:N_S], row[0:N_S, S_P:T], seen_s, ALU.add)
                        dve.tensor_tensor(t0_[0:N_S, 3, 0:N_S], row[0:N_S, S_P:T], same_neg, ALU.add)
                        dve.tensor_reduce(Me[:, 0, h:h + 1], row[:, 0:S_P], AX.X, ALU.max).then_inc(g_red, 1)
                        dve.wait_ge(g_red, h + 1)
                        dve.tensor_reduce(M[:, 0, h:h + 1], t0_[:, 0, 0:P], AX.X, ALU.max)
                        dve.tensor_reduce(M[:, 1, h:h + 1], t0_[:, 1, 0:S_P], AX.X, ALU.max)
                        dve.tensor_reduce(M[0:N_S, 2, h:h + 1], t0_[0:N_S, 2, 0:N_S], AX.X, ALU.max)
                        vo.step(dve, dve.tensor_reduce(Me[0:N_S, 1, h:h + 1], t0_[0:N_S, 3, 0:N_S], AX.X, ALU.max))
                    dve.tensor_scalar(M[:, 0:2, :], M[:, 0:2, :], 0.0, None, ALU.max)
                    dve.tensor_scalar(Me[:, 0, :], Me[:, 0, :], 0.0, None, ALU.max)
                    dve.tensor_tensor(M[0:N_S, 2, :], M[0:N_S, 2, :], m0s[:], ALU.max)
                    vo.step(dve, dve.tensor_tensor(Me[0:N_S, 1, :], Me[0:N_S, 1, :], m0s[:], ALU.max))
                    dve.tensor_tensor(dif[:, 0:3, :], nb_[:, 0:3, :], M[:], ALU.subtract)
                    dve.tensor_tensor(dif[:, 3:5, :], ga[:, 0:2, :], Me[:, 0:1, :].broadcast_to([P, 2, AH]), ALU.subtract)
                    dve.tensor_tensor(dif[0:N_S, 5, :], ga[0:N_S, 2, :], Me[0:N_S, 1, :], ALU.subtract)
                    dve.tensor_tensor(dif[0:N_S, 6, :], m0s[:], M[0:N_S, 2, :], ALU.subtract)
                    dve.tensor_tensor(m_out[:, 0, :], Me[:, 0, :], nb_[:, 3, :], ALU.subtract)
                    dve.tensor_tensor(m_out[:, 1, :], Me[:, 1, :], nb_[:, 4, :], ALU.subtract)
                    dve.tensor_tensor(dif[0:N_S, 7, :], m0s[:], Me[0:N_S, 1, :], ALU.subtract).then_inc(g_cp, 1)
                    dve.wait_ge(g_act, 5)
                    dve.tensor_copy(gem[:], dif[:, 0:3, :])
                    dve.tensor_copy(gwk[:], dif[:, 3:6, :])
                    dve.tensor_copy(gws[:], dif[0:N_S, 6, :])
                    dve.tensor_tensor(decm[:], dif[0:N_S, 7, :].unsqueeze(1).broadcast_to([N_S, NB, AH]),
                                      C("first_of_b").unsqueeze(2).broadcast_to([N_S, NB, AH]), ALU.mult).then_inc(g_a, 1)
                    dve.wait_ge(g_pe, 5)
                    dve.tensor_copy(decb[:].rearrange("p b h -> p (b h)"), bank[1][:, 0:NB * AH])

        with ExitStack() as ph:
            qT_ = sb(ph, "qT_m", [P, 2, T])
            kT_ = sb(ph, "kT_m", [P, 2, T])
            vT_ = sb(ph, "vT_m", [P, 2, T])
            so = sb(ph, "so", [P, 2, T])
            kw = sb(ph, "kw", [P, 3, DQK])
            vt = sb(ph, "vt", [P, 3, DVE_ + 1])
            W = sb(ph, "W", [P, 416])
            sc_ = sb(ph, "sc_m", [P, 416])
            nmr = sb(ph, "nmr", [AH, T])
            qm = sb(ph, "qm", [P, NB, N_S])
            km = sb(ph, "km", [N_S, NB, DQK])
            Cs = sb(ph, "Cs", [P, 2, NB, DVE_])
            Cp = sb(ph, "Cp", [P, 2, DVE_])
            dws = sb(ph, "dws", [N_S, DVE_])
            ns = sb(ph, "ns", [N_S, DVE_])
            dn = sb(ph, "dn", [P, 3])
            ssm = sb(ph, "ssm", [P, 3])
            hn = sb(ph, "hn", [P, 3, DV])
            sqm = sb(ph, "sqm", [P, 3, DV])
            yh = sb(ph, "yh", [P, 2, T])
            n_tr = sb(ph, "n_tr", [AH + NB * AH, P])
            names = ("t kw vc0 vc1 nmr nm w ex sc qm km num ds dn rd hn sq rt r2 hs ht y H L cp cpe cs csu nc ncp nall one fin").split()
            H = {x: sem("h_" + x) for x in names}
            c_in = [sem("c_in0"), sem("c_in1")]
            c_out = [sem("c_out0"), sem("c_out1")]
            cp_out = [sem("cp_out0"), sem("cp_out1")]
            seen_t, seen_t_s = C("seen_t"), C("seen_t_s")
            LAST = AH - 1

            def read_out(eng, h, j):
                n = At(N0 + 6 * h.c + j, 6 * h.step, h.i)
                eng.wait_ge(z_free[n.mod(4)], n.div(4, 1))

            def head_pairs(eng, body):
                body(At(0), At(N0), True, False)
                with eng.Fori(0, (AH - 2) // 2) as i:
                    for s in range(2):
                        body(At(1 + s, 2, i), At(N0 + 6 * (1 + s), 12, i), True, True)
                body(At(LAST), At(N0 + 6 * LAST), True, True)
                body(At(AH), None, False, True)

            with nc.Block() as blk:
                @blk.sync
                def _(sp):
                    def heads_(h, n, blocks, chain):
                        if not blocks:
                            return
                        a = h.mod(2)
                        need(sp, c_out[a], h.div(2, 0, 16))
                        sp.dma_start(Cs[:, a, :, 0:DV], A["state_mlstm_C"][0][:, bass.ds(h.of(), 1)].rearrange("b o d v -> d (b o) v")).then_inc(c_in[a], 16)
                        head_load(sp, h, 4)
                        head_load(sp, h, 5)
                        for m in range(4):
                            if n.i is None and h.c == LAST:
                                branch_load(sp, At(0), m, N0 + 6 * AH, wa_v, O_GA)
                            else:
                                head_load(sp, h + 1, m)
                    head_pairs(sp, heads_)
                    sp.wait_ge(H["fin"], 1)
                    store(sp, O["mlstm_n_p"][0, 0], n_tr[0:AH, :])
                    store(sp, O["mlstm_n_s"][0].rearrange("b h d -> (b h) d"), n_tr[AH:, :])
                    all_stored(sp)

                @blk.tensor
                def _(pe):
                    def step(h, j):
                        a = h.mod(2)
                        if j == 0:
                            read_out(pe, h, 2)
                            need(pe, H["y"], h.of(2))
                            for t, (q0, n) in enumerate(TILES):
                                tr = pe.transpose(bank[4][0:n, t * P:(t + 1) * P], kT_[:, a, q0:q0 + n], ident)
                            tr.then_inc(H["t"], 1)
                            for t, (q0, n) in enumerate(TILES):
                                tr = pe.transpose(bank[5][0:n, t * P:(t + 1) * P], vT_[:, 0, q0:q0 + n], ident)
                            tr.then_inc(H["t"], 1)
                        if j == 1:
                            pe.wait_ge(H["kw"], h.of(3, 3))
                            read_out(pe, h, 3)
                            for t, (q0, n) in enumerate(TILES):
                                tr = pe.transpose(bank[4][0:n, t * P:(t + 1) * P], vT_[:, 1, q0:q0 + n], ident)
                            tr.then_inc(H["t"], 1)
                            pe.wait_ge(H["vc0"], h.of(2, 2))
                            pe.matmul(bank[5][:, 0:S_P], kT_[:, a, 0:P], qT_[:, a, 0:S_P], start=True, stop=True)
                            pe.matmul(bank[5][:, S_P:3 * P], kT_[:, a, P:S_P], qT_[:, a, P:S_P], start=True, stop=True)
                            pe.matmul(bank[5][0:N_S, 3 * P:3 * P + N_S], kT_[:, a, S_P:], qT_[:, a, S_P:], start=True, stop=True)
                            pe.wait_ge(H["nmr"], h.of(1, 1))
                            need(pe, H["csu"], h.of(NB))
                            pe.matmul(bank[6][:, 0:T], ones[0:AH, :], nmr[:], start=True, stop=True).then_inc(H["nm"], 1)
                        if j == 2:
                            pe.wait_ge(H["vc1"], h.of(2, 2))
                            pe.wait_ge(H["sc"], h.of(2, 2))
                            pe.wait_ge(H["qm"], h.of(1, 1))
                            pe.wait_ge(c_in[a], h.div(2, 1, 16))
                            pe.wait_ge(H["nc"], h.of(1, 1))
                            pe.matmul(bank[4][:, 0:DVE_], sc_[:, 0:P], vt[:, 0, 0:DVE_], start=True, stop=True)
                            pe.matmul(bank[6][:, 0:DVE_], sc_[:, P:S_P], vt[:, 0, 0:DVE_], start=True, stop=False)
                            pe.matmul(bank[6][:, 0:DVE_], sc_[:, S_P:3 * P], vt[:, 1, 0:DVE_], start=False, stop=True)
                            pe.matmul(bank[7][0:N_S, 0:DVE_], sc_[0:N_S, 3 * P:3 * P + N_S], vt[0:N_S, 2, 0:DVE_], start=True, stop=True)
                            for b in range(NB):
                                mm = pe.matmul(bank[5][0:N_S, 0:DVE_], qm[:, b, :], Cs[:, a, b, :], start=b == 0, stop=b == NB - 1)
                            mm.then_inc(H["num"], 1)
                        if j == 3:
                            pe.wait_ge(H["hs"], h.of(3, 3))
                            for c in range(2):
                                for t, (q0, n) in enumerate(TILES):
                                    tr = pe.transpose(bank[4 + c][:, q0:q0 + n], hn[0:n, t, c * P:(c + 1) * P], ident[0:n, 0:n])
                                tr.then_inc(H["ht"], 1)
                            for t in range(2):
                                mm = pe.matmul(bank[6][:, 0:DVE_], kw[:, t, :], vt[:, t, 0:DVE_], start=t == 0, stop=t == 1)
                            mm.then_inc(H["cp"], 1)
                        if j >= 4:
                            for b in range((j - 4) * 4, (j - 3) * 4):
                                if b == 0:
                                    pe.wait_ge(H["km"], h.of(1, 1))
                                    pe.wait_ge(H["cpe"], h.of(1, 1))
                                if b >= 2:
                                    pe.wait_ge(H["csu"], h.of(NB, b - 1))
                                pe.matmul(bank[7 - b % 2][:, 0:DVE_], km[:, b, :], vt[0:N_S, 2, 0:DVE_], start=True, stop=True).then_inc(H["cs"], 1)

                    def heads_(h, n, blocks, chain):
                        for j in range(6):
                            if blocks:
                                block(pe, n + j, n + j, lambda k: xnH[:, k, :], lambda k: xnL[:, k, :])
                            if chain:
                                step(h - 1, j)
                    head_pairs(pe, heads_)
                    pe.wait_ge(H["ncp"], AH)
                    pe.wait_ge(H["nall"], AH)
                    pe.transpose(bank[4][0:AH + NB * AH, 0:P], n_all[:], ident).then_inc(H["t"], 1)

                @blk.scalar
                def _(act):
                    def evac(h, n, j):
                        a = h.mod(2)
                        z = bank[n.mod(4)][:, 0:T]
                        act.wait_ge(w_done, n.of(1, 1))
                        if j == 0:
                            need(act, H["num"], h.of(1, -1))
                            need(act, H["qm"], h.of(1, -1))
                            ins = act.activation(qT_[:, a, :], z, ACT.Copy)
                        elif j == 1:
                            ins = act.activation(kT_[:, a, :], z, ACT.Copy, scale=DQK ** -0.5)
                        elif j < 4:
                            need(act, H["t"], h.of(3))
                            ins = act.activation(vT_[:, j - 2, :], z, ACT.Copy)
                        else:
                            need(act, H["y"], h.of(2))
                            ins = act.activation(so[:, j - 4, :], z, ACT.Sigmoid)
                        ins.then_inc(z_free[n.mod(4)], 1)

                    def values(h, c, which):
                        b = bank[5 - c][:, 0:3 * P].rearrange("p (t d) -> p t d", t=3)
                        act.activation(vt[:, 0:2, c * P:(c + 1) * P], b[:, 0:2, :], ACT.Copy).then_inc(H[which], 1)
                        act.activation(vt[0:N_S, 2, c * P:(c + 1) * P], b[0:N_S, 2, :], ACT.Copy).then_inc(H[which], 1)

                    def step(h, j):
                        a = h.mod(2)
                        if j == 0:
                            act.wait_ge(H["t"], h.of(3, 2))
                            need(act, H["cs"], h.of(NB))
                            values(h, 0, "vc0")
                            need(act, H["nm"], h.of())
                            act.activation(nmr[:], neg_MT[:], ACT.Copy, scale=ident[0:AH, bass.ds(h.of(), 1)]).then_inc(H["nmr"], 1)
                        if j == 1:
                            act.wait_ge(H["t"], h.of(3, 3))
                            values(h, 1, "vc1")
                            act.wait_ge(H["w"], h.of(3, 3))
                            act.activation(W[:, 0:3 * P], W[:, 0:3 * P], ACT.Exp).then_inc(H["ex"], 1)
                            act.activation(W[0:N_S, 3 * P:], W[0:N_S, 3 * P:], ACT.Exp).then_inc(H["ex"], 1)
                        if j == 2:
                            act.wait_ge(H["num"], h.of(1, 1))
                            need(act, H["dn"], h.of(7))
                            act.activation(dws[:], bank[5][0:N_S, 0:DVE_], ACT.Copy, scale=gws[:, bass.ds(h.of(), 1)]).then_inc(H["ds"], 1)
                            for t in range(3):
                                n = TILES[t][1]
                                act.wait_ge(H["hn"], h.of(3, t + 1))
                                need(act, H["sq"], h.of(3))
                                act.activation(sqm[0:n, t, :], hn[0:n, t, :], ACT.Square, accum_out=ssm[0:n, t:t + 1]).then_inc(H["sq"], 1)
                            act.wait_ge(H["sq"], h.of(3, 3))
                            act.activation(ssm[:], ssm[:], ACT.Sqrt, scale=1.0 / DV, bias=eps).then_inc(H["rt"], 1)
                        if j == 3:
                            for c in range(2):
                                act.wait_ge(H["y"], h.of(2, c + 1))
                                act.activation(haH[:, bass.ds(h.of(2, c), 1), :].rearrange("p o t -> p (o t)"), yh[:, c, :], ACT.Copy).then_inc(H["H"], 1)
                            act.wait_ge(H["cp"], h.of(1, 1))
                            need(act, cp_out[a], h.div(2, 0, 16))
                            act.activation(Cp[:, a, :], bank[6][:, 0:DVE_], ACT.Copy).then_inc(H["cpe"], 1)
                            act.wait_ge(H["cpe"], h.of(1, 1))
                            act.dma_start(O["mlstm_C_p"][0, 0, bass.ds(h.of(), 1)].rearrange("o d v -> (o d) v"), Cp[:, a, 0:DV]).then_inc(cp_out[a], 16)
                            act.activation(n_all[:, bass.ds(h.of(), 1)], Cp[:, a, DV:], ACT.Copy).then_inc(H["nall"], 1)
                        if j == 5:
                            act.wait_ge(H["csu"], h.of(NB, NB))
                            act.dma_start(O["mlstm_C_s"][0][:, bass.ds(h.of(), 1)].rearrange("b o d v -> d (b o) v"), Cs[:, a, :, 0:DV]).then_inc(c_out[a], 16)

                    def heads_(h, n, blocks, chain):
                        for j in range(6):
                            if blocks:
                                split_hi(act, n + (j + 1))
                                evac(h, n + j, j)
                            if chain:
                                step(h - 1, j)
                    split_hi(act, At(N0))
                    head_pairs(act, heads_)
                    for a in range(2):
                        act.wait_ge(c_out[a], 8 * AH)
                        act.wait_ge(cp_out[a], 8 * AH)

                @blk.gpsimd
                def _(pool):
                    def step(h, j):
                        if j == 0:
                            a = h.mod(2)
                            read_out(pool, h, 0)
                            need(pool, H["num"], h.of())
                            pool.tensor_tensor(qm[:], qT_[:, a, S_P:].unsqueeze(1).broadcast_to([P, NB, N_S]),
                                               C("cols_of_b").rearrange("p (b s) -> p b s", b=NB), ALU.mult).then_inc(H["qm"], 1)
                            pool.wait_ge(H["kw"], h.of(3, 3))
                            need(pool, H["cs"], h.of(NB))
                            pool.tensor_tensor(km[:], kw[0:N_S, 2, :].unsqueeze(1).broadcast_to([N_S, NB, DQK]),
                                               C("of_b").unsqueeze(2).broadcast_to([N_S, NB, DQK]), ALU.mult).then_inc(H["km"], 1)

                    def heads_(h, n, blocks, chain):
                        if chain:
                            step(h - 1, 0)
                    head_pairs(pool, heads_)

                @blk.vector
                def _(dve):
                    def step(h, j):
                        a = h.mod(2)
                        col = bass.ds(h.of(), 1)
                        if j == 0:
                            dve.wait_ge(H["t"], h.of(3, 1))
                            need(dve, H["cp"], h.of())
                            need(dve, H["km"], h.of())
                            for t, (q0, n) in enumerate(TILES):
                                dve.tensor_scalar(kw[0:n, t, :], bank[4][0:n, t * P:(t + 1) * P], gwk[0:n, t, col], None, ALU.mult).then_inc(H["kw"], 1)
                            dve.wait_ge(c_in[a], h.div(2, 1, 16))
                            dve.tensor_copy(Cs[:, a, :, DV:].rearrange("p b o -> p (b o)"), nT[:, :, col].rearrange("p b o -> p (b o)")).then_inc(H["nc"], 1)
                        if j == 1:
                            dve.wait_ge(H["nm"], h.of(1, 1))
                            nm_ = bank[6]
                            dve.scalar_tensor_tensor(W[:, 0:S_P], nm_[:, 0:S_P], ga[:, 0, col], seen_t, ALU.add, ALU.min).then_inc(H["w"], 1)
                            dve.scalar_tensor_tensor(W[:, S_P:3 * P], nm_[:, P:S_P], ga[:, 1, col], seen_t[:, 0:P], ALU.add, ALU.min).then_inc(H["w"], 1)
                            dve.scalar_tensor_tensor(W[0:N_S, 3 * P:], nm_[0:N_S, S_P:T], ga[0:N_S, 2, col], seen_t_s, ALU.add, ALU.min).then_inc(H["w"], 1)
                            dve.wait_ge(H["ex"], h.of(2, 2))
                            dve.tensor_tensor(sc_[:, 0:3 * P], bank[5][:, 0:3 * P], W[:, 0:3 * P], ALU.mult).then_inc(H["sc"], 1)
                            dve.tensor_tensor(sc_[0:N_S, 3 * P:], bank[5][0:N_S, 3 * P:3 * P + N_S], W[0:N_S, 3 * P:], ALU.mult).then_inc(H["sc"], 1)
                        if j == 2:
                            dve.wait_ge(H["ds"], h.of(1, 1))
                            dve.tensor_tensor(ns[:], bank[7][0:N_S, 0:DVE_], dws[:], ALU.add).then_inc(H["dn"], 1)
                            dve.wait_ge(H["dn"], h.of(7, 1))
                            srcs = (bank[4], bank[6], ns)
                            for t, (q0, n) in enumerate(TILES):
                                dve.tensor_scalar(dn[0:n, t:t + 1], srcs[t][0:n, DV:DVE_], -1.0, gem[0:n, t, col], ALU.mult, ALU.max).then_inc(H["dn"], 1)
                            dve.wait_ge(H["dn"], h.of(7, 4))
                            for t, (q0, n) in enumerate(TILES):
                                dve.tensor_tensor(dn[0:n, t:t + 1], dn[0:n, t:t + 1], srcs[t][0:n, DV:DVE_], ALU.max).then_inc(H["dn"], 1)
                            dve.wait_ge(H["dn"], h.of(7, 7))
                            dve.reciprocal(dn[:], dn[:]).then_inc(H["rd"], 1)
                            dve.wait_ge(H["rd"], h.of(1, 1))
                            for t, (q0, n) in enumerate(TILES):
                                dve.tensor_scalar(hn[0:n, t, :], srcs[t][0:n, 0:DV], dn[0:n, t:t + 1], None, ALU.mult).then_inc(H["hn"], 1)
                            dve.wait_ge(H["rt"], h.of(1, 1))
                            dve.reciprocal(ssm[:], ssm[:]).then_inc(H["r2"], 1)
                            dve.wait_ge(H["r2"], h.of(1, 1))
                            for t, (q0, n) in enumerate(TILES):
                                dve.tensor_scalar(hn[0:n, t, :], hn[0:n, t, :], ssm[0:n, t:t + 1], None, ALU.mult).then_inc(H["hs"], 1)
                        if j == 3:
                            for c in range(2):
                                dve.wait_ge(H["ht"], h.of(2, c + 1))
                                read_out(dve, h, 5)
                                need(dve, H["L"], h.of(2))
                                dve.scalar_tensor_tensor(yh[:, c, :], bank[4 + c][:, 0:T], vec[:, bass.ds(h.of(2, G_ML + c), 1)], so[:, c, :],
                                                         ALU.mult, ALU.mult).then_inc(H["y"], 1)
                            for c in range(2):
                                dve.wait_ge(H["H"], h.of(2, c + 1))
                                at = bass.ds(h.of(2, c), 1)
                                dve.tensor_tensor(haL[:, at, :].rearrange("p o t -> p (o t)"), yh[:, c, :],
                                                  haH[:, at, :].rearrange("p o t -> p (o t)").bitcast(F32), ALU.subtract).then_inc(H["L"], 1)
                        if j >= 4:
                            for b in range((j - 4) * 4, (j - 3) * 4):
                                dve.wait_ge(H["cs"], h.of(NB, b + 1))
                                c_ = Cs[:, a, b, :]
                                dve.scalar_tensor_tensor(c_, c_, decb[:, b, col], bank[7 - b % 2][:, 0:DVE_], ALU.mult, ALU.add).then_inc(H["csu"], 1)
                        if j == 5:
                            dve.wait_ge(H["csu"], h.of(NB, NB))
                            dve.tensor_copy(n_all[:, AH:].rearrange("p (b h) -> p b h", h=AH)[:, :, col].rearrange("p b o -> p (b o)"),
                                            Cs[:, a, :, DV:].rearrange("p b o -> p (b o)")).then_inc(H["ncp"], 1)

                    def heads_(h, n, blocks, chain):
                        for j in range(6):
                            if blocks:
                                split_lo(dve, n + (j + 1))
                            if chain:
                                step(h - 1, j)
                    dve.memset(vt[:, :, DV:], 1.0).then_inc(H["one"], 1)
                    dve.memset(dn[:], 1.0).then_inc(H["one"], 1)
                    dve.memset(ssm[:], 1.0).then_inc(H["one"], 1)
                    dve.wait_ge(H["one"], 3)
                    split_lo(dve, At(N0))
                    head_pairs(dve, heads_)
                    dve.wait_ge(H["t"], 3 * AH + 1)
                    dve.tensor_copy(n_tr[:], bank[4][0:AH + NB * AH, 0:P]).then_inc(H["fin"], 1)
        hd.close()
        recycle()

        hT = sb(ctx, "hT", [P, KC, T])
        N_A = N0 + 6 * AH
        N_B = N_A + 2 * KC
        N_O = N_B + 2 * KC
        N_U = N_O + KC
        HC = 4

        def chunk(t, c):
            return t[:, bass.ds(c.of(), 1), :].rearrange("p o t -> p (o t)")

        def out_load(sp, c, m):
            w_load(sp, c + (N_O + m), wo_v, c.of(P, m * P))

        def chunk_loop(eng, body, n, per):
            with eng.Fori(0, n // per - 1) as i:
                body(At(0, per, i))
            body(At(n - per))

        def branch(n0, view, gate, first, next_load, prelude, sp_end, tag):
            with ExitStack() as ph:
                sg = sb(ph, "sg" + tag, [P, 2, T])
                br = sb(ph, "br" + tag, [P, 2, T])
                b_m, b_a, b_h, b_l = (sem(x + tag) for x in ("b_m", "b_a", "b_h", "b_l"))
                pieces = prelude(ph)

                def at(c, m):
                    return At(n0 + 2 * c.c + m, 2 * c.step, c.i)

                with nc.Block() as blk:
                    @blk.sync
                    def _(sp):
                        pieces["sync"](sp)

                        def body(c):
                            for m in range(4):
                                if c.i is None and c.c == KC - 2:
                                    next_load(sp, m)
                                else:
                                    branch_load(sp, c + 2, m, n0, view, gate)
                        chunk_loop(sp, body, KC, 2)
                        sp_end(sp)

                    @blk.tensor
                    def _(pe):
                        pieces["tensor"](pe)

                        def body(c):
                            for m in range(4):
                                H_, L_ = (xnH, xnL) if m % 2 else (haH, haL)
                                block(pe, at(c, m), at(c, m), lambda k: H_[:, k, :], lambda k: L_[:, k, :])
                        chunk_loop(pe, body, KC, 2)

                    @blk.scalar
                    def _(act):
                        pieces["scalar"](act)

                        def body(c):
                            for m in range(4):
                                split_hi(act, at(c, m + 1))
                                if m % 2:
                                    n = at(c, m)
                                    act.wait_ge(w_done, n.of(1, 1))
                                    need(act, z_free[at(c, m - 1).mod(4)], at(c, m - 1).div(4))
                                    act.activation(sg[:, m // 2, :], bank[n.mod(4)][:, 0:T], ACT.Sigmoid).then_inc(z_free[n.mod(4)], 1)
                        chunk_loop(act, body, KC, 2)
                        if not first:
                            for c in range(KC):
                                act.wait_ge(b_a, c + 1)
                                act.activation(haH[:, c, :], hT[:, c, :], ACT.Copy).then_inc(b_h, 1)

                    @blk.vector
                    def _(dve):
                        pieces["vector"](dve)

                        def body(c):
                            for m in range(4):
                                split_lo(dve, at(c, m + 1))
                                if m % 2:
                                    z, g = at(c, m - 1), at(c, m)
                                    dve.wait_ge(z_free[g.mod(4)], g.div(4, 1))
                                    dst = chunk(hT, c + m // 2) if first else br[:, m // 2, :]
                                    dve.tensor_tensor(dst, bank[z.mod(4)][:, 0:T], sg[:, m // 2, :], ALU.mult).then_inc(z_free[z.mod(4)], 1)
                                    if not first:
                                        dve.wait_ge(z_free[z.mod(4)], z.div(4, 1))
                                        h_ = chunk(hT, c + m // 2)
                                        dve.tensor_tensor(h_, h_, br[:, m // 2, :], ALU.add).then_inc(b_a, 1)
                        chunk_loop(dve, body, KC, 2)
                        if not first:
                            for c in range(KC):
                                dve.wait_ge(b_h, c + 1)
                                dve.tensor_tensor(haL[:, c, :], hT[:, c, :], haH[:, c, :].bitcast(F32), ALU.subtract).then_inc(b_l, 1)

        def nothing(ph):
            return {x: (lambda eng: None) for x in ("sync", "tensor", "scalar", "vector")}

        branch(N_A, wa_v, O_GA, True, lambda sp, m: branch_load(sp, At(0), m, N_B, wb_v, O_GB), nothing, lambda sp: None, "_a")

        def attention_parts(ph):
            hb = sb(ph, "hb", [P, 2, HC, T])
            hb_in, hb_h, hb_l = [sem("hb_in0"), sem("hb_in1")], sem("hb_h"), sem("hb_l")

            def load(sp):
                for q in range(BH // HC):
                    need(sp, hb_l, q - 1)
                    sp.dma_start(hb[:, q % 2], hb_dram[:, q * HC:(q + 1) * HC, :]).then_inc(hb_in[q % 2], 16)

            def hi(act):
                for q in range(BH // HC):
                    act.wait_ge(hb_in[q % 2], 16 * (q // 2 + 1))
                    act.activation(haH[:, q * HC:(q + 1) * HC, :], hb[:, q % 2], ACT.Copy).then_inc(hb_h, 1)

            def lo(dve):
                for q in range(BH // HC):
                    dve.wait_ge(hb_h, q + 1)
                    dve.tensor_tensor(haL[:, q * HC:(q + 1) * HC, :], hb[:, q % 2], haH[:, q * HC:(q + 1) * HC, :].bitcast(F32),
                                      ALU.subtract).then_inc(hb_l, 1)
            return {"sync": load, "tensor": lambda pe: pe.wait_ge(hb_l, BH // HC), "scalar": hi, "vector": lo}

        branch(N_B, wb_v, O_GB, False, lambda sp, m: out_load(sp, At(0), m), attention_parts, lambda sp: None, "_b")

        CR = 2 * NB + CW + 1
        QF = 2 * FC // 4
        cv = sb(ctx, "cv", [P, 2 * FC, CR + 2])
        with ExitStack() as ph:
            xb = sb(ph, "xb", [P, 2, T])
            rin = sb(ph, "rin", [CR, 2, QF * P])
            rin_in, r_t, r_ev = [sem("rin_in0"), sem("rin_in1")], sem("r_t"), sem("r_ev")
            xb_in = [sem("xb_in0"), sem("xb_in1")]

            def up_load(sp, g, j, m):
                base = N_U + g * (2 * GRP + 2 * KC)
                w_load(sp, At(base + 2 * j.c + m, 2 * j.step, j.i), up_v, j.of(P, (g * GRP + m // 2) * P + m % 2 * FF))

            with nc.Block() as blk:
                @blk.sync
                def _(sp):
                    def rows(q):
                        need(sp, r_t, q - 1)
                        cols = slice(q * QF * P, (q + 1) * QF * P)
                        sp.dma_start(rin[0:2 * NB, q % 2, :], A["state_conv"][0].rearrange("b r f -> (b r) f")[:, cols]).then_inc(rin_in[q % 2], 16)
                        sp.dma_start(rin[2 * NB:2 * NB + CW, q % 2, :], A["w_conv"][0][:, cols]).then_inc(rin_in[q % 2], 16)
                        sp.dma_start(rin[CR - 1:CR, q % 2, :], A["b_conv"][:, cols]).then_inc(rin_in[q % 2], 16)

                    def body(c):
                        for m in range(4):
                            if c.i is None and c.c == KC - 4:
                                up_load(sp, 0, At(0), m)
                            else:
                                out_load(sp, c + 4, m)
                            a = m % 2
                            if c.i is not None or c.c + m >= 2:
                                n = c + (N_O + m - 2)
                                sp.wait_ge(z_free[n.mod(4)], n.div(4, 1))
                            sp.dma_start(xb[:, a, :], xT_dram[:, bass.ds(c.of(1, m), 1), :].rearrange("p o t -> p (o t)")).then_inc(xb_in[a], 16)
                    rows(0)
                    rows(1)
                    body(At(0))
                    rows(2)
                    rows(3)
                    with sp.Fori(1, KC // 4 - 1) as i:
                        body(At(0, 4, i))
                    body(At(KC - 4))

                @blk.tensor
                def _(pe):
                    def body(c):
                        for m in range(4):
                            n = c + (N_O + m)
                            block(pe, n, n, lambda k: haH[:, k, :], lambda k: haL[:, k, :])

                    def rows(q):
                        pe.wait_ge(rin_in[q % 2], 48 * (q // 2 + 1))
                        for k in range(QF):
                            tr = pe.transpose(bank[4 + q][:, k * CR:(k + 1) * CR], rin[:, q % 2, k * P:(k + 1) * P], ident[0:CR, 0:CR])
                        tr.then_inc(r_t, 1)
                    body(At(0))
                    rows(0)
                    rows(1)
                    with pe.Fori(1, KC // 4 - 1) as i:
                        body(At(0, 4, i))
                    rows(2)
                    rows(3)
                    body(At(KC - 4))

                @blk.scalar
                def _(act):
                    def body(c):
                        for m in range(4):
                            split_hi(act, c + (N_O + m + 1))
                    with act.Fori(0, KC // 4) as i:
                        body(At(0, 4, i))
                    for q in range(4):
                        act.wait_ge(r_t, q + 1)
                        act.activation(cv[:, q * QF:(q + 1) * QF, 0:CR], bank[4 + q][:, 0:QF * CR].rearrange("p (k r) -> p k r", r=CR),
                                       ACT.Copy).then_inc(r_ev, 1)

                @blk.vector
                def _(dve):
                    def body(c):
                        for m in range(4):
                            n = c + (N_O + m)
                            split_lo(dve, n + 1)
                            dve.wait_ge(w_done, n.of(1, 1))
                            dve.wait_ge(xb_in[m % 2], c.of(8, (m // 2 + 1) * 16))
                            dve.tensor_tensor(chunk(hT, c + m), bank[n.mod(4)][:, 0:T], xb[:, m % 2, :], ALU.add).then_inc(z_free[n.mod(4)], 1)
                    with dve.Fori(0, KC // 4) as i:
                        body(At(0, 4, i))

        with ExitStack() as ph:
            nf = norm(norm_parts(ph, "_f"), hT, KC, G_FFN, bank[7], xnH, xnL)
            with nc.Block() as blk:
                @blk.tensor
                def _(pe):
                    nf.tensor(pe)

                @blk.scalar
                def _(act):
                    nf.scalar(act)

                @blk.vector
                def _(dve):
                    nf.vector(dve)

        EXT = 2 + S_P + NB * (2 + S_S)
        CE = EXT - 2
        NX = GRP - KC
        PER_G = 2 * GRP + 2 * KC
        with ExitStack() as ph:
            axH = sb(ph, "axH", [P, NX, T], F32R)
            axL = sb(ph, "axL", [P, NX, T], F32R)
            e = sb(ph, "e", [P, 2, 2, EXT])
            cc = sb(ph, "cc", [P, 2, 2, EXT])
            sg = sb(ph, "sg_f", [P, 2, CE])
            a32 = sb(ph, "a32", [P, 2, T])
            (u_zero, u_prev, u_new, u_id, u_cv, u_sg, u_g, u_a, u_H, u_L) = (
                sem("u_" + x) for x in ("zero", "prev", "new", "id", "cv", "sg", "g", "a", "H", "L"))

            def samples(t, width=2 + S_S):
                return t[:, 2 + S_P:2 + S_P + NB * width].rearrange("p (b s) -> p b s", b=NB)

            def up_at(g, j, m):
                return At(N_U + PER_G * g + 2 * j.c + m, 2 * j.step, j.i)

            def up_count(g, j, m):
                return At(2 * GRP * g + 2 * j.c + m, 2 * j.step, j.i)

            def conv_row(g, j, m):
                return j.of(1, g * GRP + m // 2 + m % 2 * FC)

            def down_load(sp, g, c, m):
                n = At(N_U + PER_G * g + 2 * GRP + 2 * c.c + m, 2 * c.step, c.i)
                w_load(sp, n, down_v, c.of(P, m // 2 * P), k0=g * GRP + m % 2 * KD, kc=KD)

            def up_bodies(eng, body):
                body(At(0))
                with eng.Fori(1, KC // 2) as i:
                    body(At(0, 2, i))
                with eng.Fori(KC // 2, GRP // 2 - 1) as i:
                    body(At(0, 2, i), True)
                body(At(GRP - 2), True)

            def act_chunk(j, beyond, dst, ext):
                return chunk(ext, j - KC) if beyond else chunk(dst, j)

            with nc.Block() as blk:
                @blk.sync
                def _(sp):
                    for g in range(2):
                        def up(j, beyond=False):
                            for m in range(4):
                                if j.i is None and j.c == GRP - 2:
                                    down_load(sp, g, At(0), m)
                                else:
                                    up_load(sp, g, j + 2, m)
                        up_bodies(sp, up)

                        def down(c):
                            for m in range(4):
                                if c.i is not None:
                                    down_load(sp, g, c + 2, m)
                                elif g == 0:
                                    up_load(sp, 1, At(0), m)
                        chunk_loop(sp, down, KC, 2)

                @blk.tensor
                def _(pe):
                    for g in range(2):
                        def up(j, beyond=False):
                            for m in range(4):
                                n = up_at(g, j, m)
                                block(pe, n, n, lambda k: xnH[:, k, :], lambda k: xnL[:, k, :])
                        up_bodies(pe, up)
                        pe.wait_ge(u_L, GRP * (g + 1))

                        def down(c):
                            for m in range(4):
                                n = At(N_U + PER_G * g + 2 * GRP + 2 * c.c + m, 2 * c.step, c.i)
                                k0 = m % 2 * KD
                                block(pe, n, n, lambda k: haH[:, k0 + k, :] if k0 + k < KC else axH[:, k0 + k - KC, :],
                                      lambda k: haL[:, k0 + k, :] if k0 + k < KC else axL[:, k0 + k - KC, :], kc=KD)
                        chunk_loop(pe, down, KC, 2)

                @blk.scalar
                def _(act):
                    act.wait_ge(u_zero, 1)
                    for g in range(2):
                        def up(j, beyond=False):
                            for m in range(4):
                                n, u = up_at(g, j, m), up_count(g, j, m)
                                kind, a = m % 2, m // 2
                                last = m == 3 and j.i is None and j.c == GRP - 2
                                split_hi(act, n + 1, kc=KD if last else KC)
                                act.wait_ge(w_done, n.of(1, 1))
                                need(act, u_cv, u.of(2, -6))
                                need(act, u_new, u.of(1, -3))
                                z = bank[n.mod(4)]
                                act.activation(e[:, kind, a, 2:2 + S_P], z[:, 0:S_P], ACT.Copy)
                                act.activation(samples(e[:, kind, a])[:, :, 2:], z[:, S_P:T].rearrange("p (b s) -> p b s", b=NB),
                                               ACT.Copy).then_inc(z_free[n.mod(4)], 1)
                                act.wait_ge(z_free[n.mod(4)], n.div(4, 1))
                                act.wait_ge(u_prev, u.of(1, 1))
                                k = At(GRP * g + j.c + a, j.step, j.i)
                                need(act, u_a, k.of(2, -2))
                                row = bass.ds(conv_row(g, j, m), 1)
                                w2 = cv[:, row, 2 * NB + 2:2 * NB + 3].rearrange("p o r -> p (o r)")
                                bias = cv[:, row, CR - 1:CR].rearrange("p o r -> p (o r)")
                                act.activation(cc[:, kind, a, 0:CE], e[:, kind, a, 2:], ACT.Identity, scale=w2, bias=bias).then_inc(u_id, 1)
                                if m % 2:
                                    act.wait_ge(u_cv, u.of(2))
                                    act.activation(sg[:, a, :], cc[:, 0, a, 0:CE], ACT.Sigmoid).then_inc(u_sg, 1)
                                    act.wait_ge(u_a, k.of(2, 2))
                                    act.activation(act_chunk(j + a, beyond, haH, axH), a32[:, a, :], ACT.Copy).then_inc(u_H, 1)
                        up_bodies(act, up)

                        def down(c):
                            for m in range(4):
                                n = At(N_U + PER_G * g + 2 * GRP + 2 * c.c + m, 2 * c.step, c.i)
                                last = m == 3 and c.i is None
                                if not (last and g == 1):
                                    split_hi(act, n + 1, kc=KC if last else KD)
                        chunk_loop(act, down, KC, 2)

                @blk.gpsimd
                def _(pool):
                    pool.memset(e[:], 0.0).then_inc(u_zero, 1)
                    pool.wait_ge(u_zero, 1)
                    for g in range(2):
                        def up(j, beyond=False):
                            for m in range(4):
                                n, u = up_at(g, j, m), up_count(g, j, m)
                                kind, a = m % 2, m // 2
                                row = cv[:, bass.ds(conv_row(g, j, m), 1), :].rearrange("p o r -> p (o r)")
                                prev = row[:, 0:2 * NB].rearrange("p (b s) -> p b s", b=NB)
                                es = samples(e[:, kind, a])
                                need(pool, u_cv, u.of(2, -6))
                                need(pool, u_new, u.of(1, -3))
                                pool.tensor_copy(es[:, :, 0:2], prev).then_inc(u_prev, 1)
                                pool.wait_ge(u_prev, u.of(1, 1))
                                pool.wait_ge(z_free[n.mod(4)], n.div(4, 1))
                                pool.tensor_copy(row[:, CR:], e[:, kind, a, S_P:S_P + 2])
                                pool.tensor_copy(prev, es[:, :, S_S:]).then_inc(u_new, 1)
                        up_bodies(pool, up)

                @blk.vector
                def _(dve):
                    for g in range(2):
                        def up(j, beyond=False):
                            for m in range(4):
                                n, u = up_at(g, j, m), up_count(g, j, m)
                                kind, a = m % 2, m // 2
                                last = m == 3 and j.i is None and j.c == GRP - 2
                                split_lo(dve, n + 1, kc=KD if last else KC)
                                row = bass.ds(conv_row(g, j, m), 1)
                                c_ = cc[:, kind, a, 0:CE]
                                dve.wait_ge(u_id, u.of(1, 1))
                                for s in range(2):
                                    tap_ = cv[:, row, 2 * NB + 1 - s:2 * NB + 2 - s].rearrange("p o r -> p (o r)")
                                    dve.scalar_tensor_tensor(c_, e[:, kind, a, 1 - s:1 - s + CE], tap_, c_, ALU.mult, ALU.add).then_inc(u_cv, 1)
                                    dve.wait_ge(u_cv, u.of(2, s + 1))
                                if m % 2:
                                    k = At(GRP * g + j.c + a, j.step, j.i)
                                    gate, val = cc[:, 0, a, :], cc[:, 1, a, :]
                                    dve.wait_ge(u_sg, k.of(1, 1))
                                    dve.tensor_tensor(gate[:, 0:CE], gate[:, 0:CE], sg[:, a, :], ALU.mult).then_inc(u_g, 1)
                                    dve.wait_ge(u_g, k.of(1, 1))
                                    need(dve, u_L, k.of(1, -1))
                                    dve.tensor_tensor(a32[:, a, 0:S_P], gate[:, 0:S_P], val[:, 0:S_P], ALU.mult).then_inc(u_a, 1)
                                    dve.tensor_tensor(a32[:, a, S_P:].rearrange("p (b s) -> p b s", b=NB), samples(gate)[:, :, 0:S_S], samples(val)[:, :, 0:S_S], ALU.mult).then_inc(u_a, 1)
                                    dve.wait_ge(u_H, k.of(1, 1))
                                    dve.tensor_tensor(act_chunk(j + a, beyond, haL, axL), a32[:, a, :],
                                                      act_chunk(j + a, beyond, haH, axH).bitcast(F32), ALU.subtract).then_inc(u_L, 1)
                        up_bodies(dve, up)

                        def down(c):
                            for m in range(4):
                                n = At(N_U + PER_G * g + 2 * GRP + 2 * c.c + m, 2 * c.step, c.i)
                                last = m == 3 and c.i is None
                                if not (last and g == 1):
                                    split_lo(dve, n + 1, kc=KC if last else KD)
                                dve.wait_ge(w_done, n.of(1, 1))
                                h_ = chunk(hT, c + m // 2)
                                dve.tensor_tensor(h_, h_, bank[n.mod(4)][:, 0:T], ALU.add).then_inc(z_free[n.mod(4)], 1)
                                dve.wait_ge(z_free[n.mod(4)], n.div(4, 1))
                        chunk_loop(dve, down, KC, 2)

        with ExitStack() as ph:
            crow = sb(ph, "crow", [CR + 2, 2, 4 * P])
            y_t, y_ev, v_t, v_ev = (sem(x) for x in ("y_t", "y_ev", "v_t", "v_ev"))
            v_out = [sem("v_out0"), sem("v_out1")]
            NQ = KC // 4
            NV = 2 * FC // 4
            y_p = O["y_prompt"][0].rearrange("(t p) d -> p t d", p=P)
            y_s = O["y_sample"].rearrange("b s d -> (b s) d")
            with nc.Block() as blk:
                @blk.tensor
                def _(pe):
                    for t, (q0, n) in enumerate(TILES):
                        for q in range(NQ):
                            i = t * NQ + q
                            if i >= 4:
                                pe.wait_ge(y_ev, i - 3)
                            for k in range(4):
                                tr = pe.transpose(bank[i % 4][0:n, k * P:(k + 1) * P], hT[:, q * 4 + k, q0:q0 + n], ident)
                            tr.then_inc(y_t, 1)
                    for i in range(NV):
                        if i >= 4:
                            pe.wait_ge(v_ev, i - 3)
                        for k in range(4):
                            tr = pe.transpose(bank[4 + i % 4][0:CR + 2, k * P:(k + 1) * P], cv[:, i * 4 + k, :], ident)
                        tr.then_inc(v_t, 1)

                @blk.scalar
                def _(act):
                    for i in range(NQ * 3):
                        n = TILES[i // NQ][1]
                        act.wait_ge(y_t, i + 1)
                        act.activation(stage[0:n, i // NQ, i % NQ * 4 * P:(i % NQ + 1) * 4 * P], bank[i % 4][0:n, :], ACT.Copy).then_inc(y_ev, 1)

                @blk.vector
                def _(dve):
                    for i in range(NV):
                        dve.wait_ge(v_t, i + 1)
                        if i >= 2:
                            dve.wait_ge(v_out[i % 2], 32 * (i // 2))
                        dve.tensor_copy(crow[:, i % 2, :], bank[4 + i % 4][0:CR + 2, :]).then_inc(v_ev, 1)

                @blk.gpsimd
                def _(pool):
                    for i in range(NV):
                        pool.wait_ge(v_ev, i + 1)
                        cols = slice(i * 4 * P, (i + 1) * 4 * P)
                        pool.dma_start(O["conv_s"][0].rearrange("b r f -> (b r) f")[:, cols], crow[0:2 * NB, i % 2, :]).then_inc(v_out[i % 2], 16)
                        pool.dma_start(O["conv_p"][0, 0][:, cols], crow[CR:, i % 2, :]).then_inc(v_out[i % 2], 16)
                    for a in range(2):
                        pool.wait_ge(v_out[a], 16 * NV)

                @blk.sync
                def _(sp):
                    for t, (q0, n) in enumerate(TILES):
                        for q in range(NQ):
                            sp.wait_ge(y_ev, t * NQ + q + 1)
                            cols = slice(q * 4 * P, (q + 1) * 4 * P)
                            store(sp, y_s[:, cols] if t == 2 else y_p[:, t, cols], stage[0:n, t, cols])
                    all_stored(sp)


OUTPUTS = {
    "y_prompt": (1, S_P, D), "y_sample": (NB, S_S, D),
    "kv_latent_p": (1, 1, S_P, KVL), "k_rope_p": (1, 1, S_P, ROPE),
    "mlstm_C_p": (1, 1, AH, DQK, DV), "mlstm_n_p": (1, 1, AH, DQK), "mlstm_m_p": (1, 1, AH),
    "conv_p": (1, 1, CW - 1, 2 * FF),
    "kv_latent_s": (1, NB, S_S, KVL), "k_rope_s": (1, NB, S_S, ROPE),
    "mlstm_C_s": (1, NB, AH, DQK, DV), "mlstm_n_s": (1, NB, AH, DQK), "mlstm_m_s": (1, NB, AH),
    "conv_s": (1, NB, CW - 1, 2 * FF),
}


def kernel(**inputs):
    import concourse.bacc as bacc
    from concourse.bass_utils import run_bass_kernel_spmd

    nc = bacc.Bacc("TRN2", target_bir_lowering=False, num_devices=1)
    arrays, ins, outs = {}, {}, {}
    for name, value in inputs.items():
        a = np.ascontiguousarray(value)
        arrays[f"in_{name}_dram"] = a
        ins[name] = nc.dram_tensor(f"in_{name}_dram", a.shape, mybir.dt.from_np(a.dtype), kind="ExternalInput").ap()
    for i, (name, shape) in enumerate(OUTPUTS.items()):
        outs[name] = nc.dram_tensor(f"out_{i}_dram", shape, F32, kind="ExternalOutput").ap()
    build(nc, ins, outs)
    r = run_bass_kernel_spmd(nc, [arrays], core_ids=[0])
    return tuple(r.results[0][f"out_{i}_dram"] for i in range(len(OUTPUTS)))
```
